# Optimizing a Trainium2 kernel written in Bass

```python
import jax, jax.numpy as jnp
from jax import lax
import numpy as np

D_MODEL = 1024
BATCH = 1
SEQ = 2048
DEPTH = 2
DEC_BATCH = 8
DEC_SEQ = 1
PAST_LEN = 512
PAGE_SIZE = 128

N_A = DEPTH // 2
N_B = DEPTH - N_A
H_A = 4
DK_A = D_MODEL // 2 // H_A
DV_A = D_MODEL // H_A
DK_TOT = H_A * DK_A
DV_TOT = H_A * DV_A
GATE_RANK = 16
GATE_TAU = 16.0
GLA_CHUNK = 64
GLA_IN = 2 * DK_TOT + 2 * DV_TOT + GATE_RANK
HD_B = 64
H_B = D_MODEL // HD_B
D_B = H_B * HD_B
KV_OUT = 2 * D_B + H_B
Q_BLOCK = 128
EPS = 1e-6

kernel_name = "yoco_gla_fox_decoder_step"

def rms_norm(x):
    xf = x.astype(jnp.float32)
    return (xf * lax.rsqrt(jnp.mean(xf * xf, axis=-1, keepdims=True) + EPS)).astype(x.dtype)

def ada_params(c, w, b, n):
    mod = jax.nn.silu(c) @ w + b
    return jnp.split(mod[:, None, :], n, axis=-1)

def gla_scan(q, k, v, loga, s0, chunk):
    f32 = jnp.float32
    B, L, H, DK = q.shape
    DV = v.shape[-1]
    n = L // chunk

    def to_chunks(t):
        return t.astype(f32).reshape(B, n, chunk, H, t.shape[-1]).transpose(1, 0, 3, 2, 4)

    qc, kc, vc, gc = to_chunks(q), to_chunks(k), to_chunks(v), to_chunks(loga)
    causal = jnp.tril(jnp.ones((chunk, chunk), dtype=bool))[None, None, :, :, None]

    def step(s, inp):
        qi, ki, vi, gi = inp
        b = jnp.cumsum(gi, axis=2)
        diff = jnp.where(causal, b[:, :, :, None, :] - b[:, :, None, :, :], -jnp.inf)
        att = jnp.einsum('bhik,bhjk,bhijk->bhij', qi, ki, jnp.exp(diff))
        o = jnp.einsum('bhij,bhjv->bhiv', att, vi) + jnp.einsum('bhik,bhkv->bhiv', qi * jnp.exp(b), s)
        b_last = b[:, :, -1:, :]
        s_new = jnp.exp(b_last[:, :, 0, :, None]) * s + jnp.einsum('bhjk,bhjv->bhkv', ki * jnp.exp(b_last - b), vi)
        return s_new, o

    s_fin, oc = lax.scan(step, s0.astype(f32), (qc, kc, vc, gc))
    o = oc.transpose(1, 0, 3, 2, 4).reshape(B, L, H, DV)
    return o, s_fin

def gla_mixer(h, s0, w_in, w_g2, b_g, onorm, w_out, chunk):
    B, L, _ = h.shape
    proj = h @ w_in
    q, k, v, g, z = jnp.split(proj, [DK_TOT, 2 * DK_TOT, 2 * DK_TOT + DV_TOT, 2 * DK_TOT + 2 * DV_TOT], axis=-1)
    q = q.reshape(B, L, H_A, DK_A) * (DK_A ** -0.5)
    k = k.reshape(B, L, H_A, DK_A)
    v = v.reshape(B, L, H_A, DV_A)
    loga = (jax.nn.log_sigmoid((z @ w_g2 + b_g).astype(jnp.float32)) / GATE_TAU).reshape(B, L, H_A, DK_A)
    o, s = gla_scan(q, k, v, loga, s0, chunk)
    o = rms_norm(o.astype(h.dtype)) * onorm
    o = o.reshape(B, L, DV_TOT) * jax.nn.silu(g)
    return o @ w_out, s

def fox_shared_kv(x, c, kv_ada_w, kv_ada_b, w_kv, b_f, k_norm):
    B, L, _ = x.shape
    shift, scale = ada_params(c, kv_ada_w, kv_ada_b, 2)
    u = rms_norm(x) * (1 + scale) + shift
    p = u @ w_kv
    k = rms_norm(p[..., :D_B].reshape(B, L, H_B, HD_B)) * k_norm
    v = p[..., D_B:2 * D_B].reshape(B, L, H_B, HD_B)
    logf = jax.nn.log_sigmoid((p[..., 2 * D_B:] + b_f).astype(jnp.float32))
    return k, v, logf

def fox_mixer(h, k_all, v_all, f_all, past, w_in, q_norm, w_out):
    B, L, _ = h.shape
    T = k_all.shape[1]
    proj = h @ w_in
    q = rms_norm(proj[..., :D_B].reshape(B, L, H_B, HD_B)) * q_norm * (HD_B ** -0.5)
    g = proj[..., D_B:]
    f_q = f_all[:, past:]
    f_k = f_all.transpose(0, 2, 1)
    qb = Q_BLOCK if L % Q_BLOCK == 0 else L
    nb = L // qb
    kpos = jnp.arange(T)

    def block(args):
        i, q_blk, fq_blk = args
        qpos = past + i * qb + jnp.arange(qb)
        s = jnp.einsum('bqhd,bkhd->bhqk', q_blk, k_all, preferred_element_type=jnp.float32)
        s = s + fq_blk.transpose(0, 2, 1)[..., None] - f_k[:, :, None, :]
        s = jnp.where((kpos[None, :] <= qpos[:, None])[None, None], s, -jnp.inf)
        p = jax.nn.softmax(s, axis=-1)
        return jnp.einsum('bhqk,bkhd->bqhd', p.astype(v_all.dtype), v_all)

    q_blocks = q.reshape(B, nb, qb, H_B, HD_B).swapaxes(0, 1)
    fq_blocks = f_q.reshape(B, nb, qb, H_B).swapaxes(0, 1)
    o = lax.map(block, (jnp.arange(nb), q_blocks, fq_blocks))
    o = o.swapaxes(0, 1).reshape(B, L, D_B)
    return (o * jax.nn.silu(g)) @ w_out

def trunk(x, c, s_gla, k_past, v_past, logf_past, gla_chunk, ada_w, ada_b, gla_w_in, gla_w_g2, gla_b_g,
          gla_onorm, gla_w_out, kv_ada_w, kv_ada_b, w_kv, b_f, k_norm, fox_w_in, q_norm, fox_w_out):
    past = k_past.shape[1]
    new_s = []
    for layer in range(DEPTH):
        if layer == N_A:
            k_new, v_new, logf_new = fox_shared_kv(x, c, kv_ada_w, kv_ada_b, w_kv, b_f, k_norm)
            k_all = jnp.concatenate([k_past.astype(k_new.dtype), k_new], axis=1)
            v_all = jnp.concatenate([v_past.astype(v_new.dtype), v_new], axis=1)
            f_all = jnp.cumsum(jnp.concatenate([logf_past.astype(jnp.float32), logf_new], axis=1), axis=1)
        shift, scale, gate = ada_params(c, ada_w[layer], ada_b[layer], 3)
        h = rms_norm(x) * (1 + scale) + shift
        if layer < N_A:
            out, s = gla_mixer(h, s_gla[layer], gla_w_in[layer], gla_w_g2[layer], gla_b_g[layer],
                               gla_onorm[layer], gla_w_out[layer], gla_chunk)
            new_s.append(s)
        else:
            j = layer - N_A
            out = fox_mixer(h, k_all, v_all, f_all, past, fox_w_in[j], q_norm[j], fox_w_out[j])
        x = x + gate * out
    return x, jnp.stack(new_s), k_new, v_new, logf_new

def setup_inputs(seed: int = 0) -> dict:
    key = jax.random.key(seed)
    ks = jax.random.split(key, 32)
    f32 = jnp.float32
    n_pages = PAST_LEN // PAGE_SIZE
    used = DEC_BATCH * n_pages
    n_pool = used + (used + 3) // 4
    nrm = lambda k, shape, s: jax.random.normal(k, shape, f32) * s
    page_table = jax.random.permutation(ks[0], n_pool)[:used].reshape(DEC_BATCH, n_pages).astype(jnp.int32)
    return {
        "x_prompt": nrm(ks[1], (BATCH, SEQ, D_MODEL), 1.0),
        "x_sample": nrm(ks[2], (DEC_BATCH, DEC_SEQ, D_MODEL), 1.0),
        "c_prompt": nrm(ks[3], (BATCH, D_MODEL), 1.0),
        "c_sample": nrm(ks[4], (DEC_BATCH, D_MODEL), 1.0),
        "state_gla": nrm(ks[5], (N_A, DEC_BATCH, H_A, DK_A, DV_A), 1.0),
        "cache_k": nrm(ks[6], (n_pool, PAGE_SIZE, H_B, HD_B), 1.0),
        "cache_v": nrm(ks[7], (n_pool, PAGE_SIZE, H_B, HD_B), 1.0),
        "cache_logf": jax.nn.log_sigmoid(3.5 + nrm(ks[8], (n_pool, PAGE_SIZE, H_B), 1.5)),
        "page_table": page_table,
        "ada_w": nrm(ks[9], (DEPTH, D_MODEL, 3 * D_MODEL), 0.5 * D_MODEL ** -0.5),
        "ada_b": nrm(ks[10], (DEPTH, 3 * D_MODEL), 0.02),
        "gla_w_in": nrm(ks[11], (N_A, D_MODEL, GLA_IN), D_MODEL ** -0.5),
        "gla_w_g2": nrm(ks[12], (N_A, GATE_RANK, DK_TOT), GATE_RANK ** -0.5),
        "gla_b_g": nrm(ks[13], (N_A, DK_TOT), 0.1),
        "gla_onorm": 1.0 + nrm(ks[14], (N_A, DV_A), 0.02),
        "gla_w_out": nrm(ks[15], (N_A, DV_TOT, D_MODEL), DV_TOT ** -0.5),
        "kv_ada_w": nrm(ks[16], (D_MODEL, 2 * D_MODEL), 0.5 * D_MODEL ** -0.5),
        "kv_ada_b": nrm(ks[17], (2 * D_MODEL,), 0.02),
        "w_kv": nrm(ks[18], (D_MODEL, KV_OUT), D_MODEL ** -0.5),
        "b_f": jax.random.uniform(ks[19], (H_B,), f32, 1.0, 6.0),
        "k_norm": 1.0 + nrm(ks[20], (HD_B,), 0.02),
        "fox_w_in": nrm(ks[21], (N_B, D_MODEL, 2 * D_B), D_MODEL ** -0.5),
        "q_norm": 1.0 + nrm(ks[22], (N_B, HD_B), 0.02),
        "fox_w_out": nrm(ks[23], (N_B, D_B, D_MODEL), D_B ** -0.5),
    }

def reference(x_prompt, x_sample, c_prompt, c_sample, state_gla, cache_k, cache_v, cache_logf, page_table,
              ada_w, ada_b, gla_w_in, gla_w_g2, gla_b_g, gla_onorm, gla_w_out, kv_ada_w, kv_ada_b, w_kv, b_f,
              k_norm, fox_w_in, q_norm, fox_w_out):
    bp = x_prompt.shape[0]
    bs = page_table.shape[0]
    s0 = jnp.zeros((N_A, bp, H_A, DK_A, DV_A), jnp.float32)
    k0 = jnp.zeros((bp, 0, H_B, HD_B), x_prompt.dtype)
    v0 = jnp.zeros((bp, 0, H_B, HD_B), x_prompt.dtype)
    lf0 = jnp.zeros((bp, 0, H_B), jnp.float32)
    y_prompt, s_p, k_p, v_p, lf_p = trunk(
        x_prompt, c_prompt, s0, k0, v0, lf0, GLA_CHUNK, ada_w, ada_b, gla_w_in, gla_w_g2, gla_b_g,
        gla_onorm, gla_w_out, kv_ada_w, kv_ada_b, w_kv, b_f, k_norm, fox_w_in, q_norm, fox_w_out)
    k_past = cache_k[page_table].reshape(bs, -1, H_B, HD_B)
    v_past = cache_v[page_table].reshape(bs, -1, H_B, HD_B)
    lf_past = cache_logf[page_table].reshape(bs, -1, H_B)
    y_sample, s_s, k_s, v_s, lf_s = trunk(
        x_sample, c_sample, state_gla, k_past, v_past, lf_past, 1, ada_w, ada_b, gla_w_in, gla_w_g2, gla_b_g,
        gla_onorm, gla_w_out, kv_ada_w, kv_ada_b, w_kv, b_f, k_norm, fox_w_in, q_norm, fox_w_out)
    return (y_prompt, y_sample, s_p, s_s, k_p, v_p, lf_p, k_s, v_s, lf_s)


_drawn_inputs = setup_inputs


def setup_inputs(seed=0):
    import zlib

    import numpy as np

    out = dict(_drawn_inputs(seed))
    spreads = {}
    factors = {'cache_logf': 3.871, 'gla_onorm': 8.0, 'k_norm': 2.93, 'q_norm': 8.0}
    for name, (base, spread) in spreads.items():
        noise = np.random.default_rng([zlib.crc32(name.encode()), seed]).standard_normal(out[name].shape)
        drawn = base * np.exp(spread * noise) if base else spread * noise
        out[name] = __import__('jax').numpy.asarray(drawn.astype(out[name].dtype))
    for name, factor in factors.items():
        out[name] = (out[name] * factor).astype(out[name].dtype)
    return out
```

```python
from contextlib import ExitStack


import concourse.bass as bass
from concourse import mybir

P = 128
NB = 512
F32 = mybir.dt.float32
F32R = mybir.dt.float32r
BF16 = mybir.dt.bfloat16
I32 = mybir.dt.int32
ALU = mybir.AluOpType
ACT = mybir.ActivationFunctionType
AX = mybir.AxisListType
ds = bass.ds
EPS = 1e-6
GATE_TAU = 16.0
LINES = 4
HIDE = -1e30


class Names:
    pass


def col_blocks(w, j):
    return w.rearrange("(k p) n -> p k n", p=P)[:, :, ds(j * NB, NB)]


def make_constants(nc, g):
    g.ident = g.keep("ident", [P, P], F32)
    g.ident16 = g.keep("ident16", [P, P], BF16)
    g.eps = g.keep("eps", [P, 1], F32)
    g.one = g.keep("one", [P, 1], F32)
    g.keep_le = g.keep("keep_le", [P, P], F32)
    g.hide_kq = g.keep("hide_kq", [P, P], BF16)
    g.hide_qk = g.keep("hide_qk", [P, P], BF16)
    made = g.sem("const_made")
    with nc.Block() as block:
        @block.gpsimd
        def _(pool):
            fills = ((g.ident, 0.0), (g.ident16, 0.0), (g.keep_le, 1.0), (g.hide_kq, 0.0), (g.hide_qk, 0.0),
                     (g.eps, EPS), (g.one, 1.0))
            for tile, value in fills:
                pool.memset(tile[:, :], value).then_inc(made, 1)
            pool.wait_ge(made, len(fills))
            for tile in (g.ident, g.ident16):
                pool.affine_select(out=tile[:, :], in_=tile[:, :], compare_op=ALU.not_equal, fill=1.0,
                                   base=0, pattern=[[-1, P]], channel_multiplier=1).then_inc(made, 1)
            for tile, fill, sign in ((g.keep_le, 0.0, 1), (g.hide_kq, HIDE, 1), (g.hide_qk, HIDE, -1)):
                pool.affine_select(out=tile[:, :], in_=tile[:, :], compare_op=ALU.is_ge, fill=fill, base=0,
                                   pattern=[[sign, P]], channel_multiplier=-sign).then_inc(made, 1)
            pool.wait_ge(made, len(fills) + 5)


def modulation_phase(nc, g):
    D, K, NC = g.D, g.K, g.NS + 1
    sources = [(g.i.ada_w[0], g.i.ada_b[0:1, :]),
               (g.i.kv_ada_w, g.i.kv_ada_b.rearrange("(a n) -> a n", a=1)),
               (g.i.ada_w[g.NA], g.i.ada_b[g.NA:g.NA + 1, :])]
    pairs = [w.shape[1] // NB // 2 for w, _ in sources]
    with ExitStack() as st:
        sb = lambda n, s, d=F32: st.enter_context(nc.sbuf_tensor(n, s, d))
        c_rows = sb("c_rows", [NC, D])
        c_silu = sb("c_silu", [NC, D])
        cT = sb("cT", [P, K, NC])
        bias = sb("bias_rows", [NC, sum(pairs) * 2 * NB])
        w_in = [sb(f"mod_w{u}", [P, K, NB]) for u in range(2)]
        rows = [sb(f"mod_rows{u}", [NC, NB]) for u in range(2)]
        c_loaded, bias_loaded = g.sem("c_loaded"), g.sem("bias_loaded")
        c_silu_done = g.sem("c_silu_done")
        c_turned, cT_ready = g.sem("c_turned"), g.sem("cT_ready")
        w_loaded = [g.sem(f"mod_w_loaded{u}") for u in range(2)]
        w_used, rows_ready = g.sem("mod_w_used"), g.sem("mod_rows_ready")
        turned, modT_ready = g.sem("mod_turned"), g.sem("modT_ready")
        rows_stored = [g.sem(f"mod_rows_stored{u}") for u in range(2)]
        plus_one = g.sem("scale_plus_one")
        ps_rows, ps_turn = (g.bank[0], g.bank[1]), (g.bank[2], g.bank[3])
        ps_c = g.bank[4][:, 0:K * NC]

        def all_blocks(eng, body):
            base = 0
            for s, n in enumerate(pairs):
                with eng.Fori(0, n) as i:
                    for u in range(2):
                        body(s, i, u, base + i)
                base += n

        with nc.Block() as block:
            @block.sync
            def _(sp):
                sp.dma_start(c_rows[0:1, :], g.i.c_prompt).then_inc(c_loaded, 16)
                sp.dma_start(c_rows[1:NC, :], g.i.c_sample).then_inc(c_loaded, 16)
                at = 0
                for w, b in sources:
                    n = b.shape[1]
                    sp.dma_start(bias[:, at:at + n], b.broadcast_to([NC, n])).then_inc(bias_loaded, 16)
                    at += n

                def load(s, i, u, h):
                    sp.wait_ge(w_used, 2 * h + u + 1)
                    sp.dma_start(w_in[u][:, :, :], col_blocks(sources[s][0], 2 * i + u)).then_inc(w_loaded[u], 16)
                all_blocks(sp, load)

            @block.scalar
            def _(act):
                act.wait_ge(c_loaded, 32)
                act.activation(c_silu[:, :], c_rows[:, :], ACT.Silu).then_inc(c_silu_done, 1)

                def store(s, i, u, h):
                    act.wait_ge(rows_ready, 2 * h + u + 1)
                    act.dma_start(g.mods[:, ds((2 * h + u) * NB, NB)], rows[u][:, :]).then_inc(rows_stored[u], 16)
                all_blocks(act, store)
                for u in range(2):
                    act.wait_ge(rows_stored[u], 16 * (sum(pairs) + 1))

            @block.tensor
            def _(pe):
                pe.sem_inc(w_used, 2)
                pe.wait_ge(c_silu_done, 1)
                for k in range(K):
                    mm = pe.transpose(ps_c[:, k * NC:(k + 1) * NC], c_silu[:, k * P:(k + 1) * P],
                                      g.ident[0:NC, 0:NC])
                mm.then_inc(c_turned, 1)
                pe.wait_ge(cT_ready, 1)

                def project(s, i, u, h):
                    pe.wait_ge(w_loaded[u], 16 * h + 16)
                    pe.wait_ge(modT_ready, 2 * h + u + 1)
                    for k in range(K):
                        mm = pe.matmul(ps_rows[u][0:NC, :], cT[:, k, :], w_in[u][:, k, :],
                                       start=(k == 0), stop=(k == K - 1))
                    mm.then_inc(w_used, 1)
                    pe.wait_ge(rows_ready, 2 * h + u + 1)
                    for q in range(NB // P):
                        mm = pe.matmul(ps_turn[u][:, q * NC:(q + 1) * NC], rows[u][:, q * P:(q + 1) * P],
                                       g.ident[0:NC, 0:NC], start=True, stop=True)
                    mm.then_inc(turned, 1)
                all_blocks(pe, project)

            @block.vector
            def _(dve):
                dve.sem_inc(modT_ready, 2)
                for u in range(2):
                    dve.sem_inc(rows_stored[u], 16)
                dve.wait_ge(c_turned, 1)
                dve.tensor_copy(cT[:, :, :].rearrange("p k c -> p (k c)"), ps_c).then_inc(cT_ready, 1)
                dve.wait_ge(bias_loaded, 16 * len(sources))

                def finish(s, i, u, h):
                    dve.wait_ge(w_used, 2 * h + u + 3)
                    dve.wait_ge(rows_stored[u], 16 * h + 16)
                    dve.tensor_tensor(rows[u][:, :], ps_rows[u][0:NC, :], bias[:, ds((2 * h + u) * NB, NB)],
                                      ALU.add).then_inc(rows_ready, 1)
                    dve.wait_ge(turned, 2 * h + u + 1)
                    dve.tensor_copy(g.modT[:, ds((2 * h + u) * (NB // P) * NC, NB // P * NC)],
                                    ps_turn[u][:, 0:NB // P * NC]).then_inc(modT_ready, 1)
                all_blocks(dve, finish)
                dve.wait_ge(modT_ready, 2 * sum(pairs) + 2)
                for first in g.mod_scale:
                    part = g.modT[:, first * NC:(first + K) * NC]
                    dve.tensor_scalar(part, part, 1.0, None, ALU.add).then_inc(plus_one, 1)
                dve.wait_ge(plus_one, len(g.mod_scale))


XS = 4


def in_turn(eng, n, head, step, last):
    head(0, 0)
    looped = (n - 1) // XS
    if looped:
        with eng.Fori(0, looped) as h:
            for u in range(XS):
                step(h, u, h + (u + 1) // XS, (u + 1) % XS)
    for t in range(XS * looped, n - 1):
        step(t // XS, t % XS, (t + 1) // XS, (t + 1) % XS)
    last((n - 1) // XS, (n - 1) % XS)


def block_groups(eng, plan, first, upcoming, rest):
    for i, p in enumerate(plan):
        if p.blocks > 1:
            with eng.Fori(0, p.blocks - 1) as j:
                first(p, j)
                upcoming(p, j + 1)
                rest(p, j)
        first(p, p.blocks - 1)
        if i + 1 < len(plan):
            upcoming(plan[i + 1], 0)
        rest(p, p.blocks - 1)


def group(kind, w, first, blocks, out, out_s, width=NB, scale=None, norm=None, bias=None):
    p = Names()
    p.kind, p.w, p.first, p.blocks, p.out, p.out_s, p.width = kind, w, first, blocks, out, out_s, width
    p.scale, p.norm, p.bias = scale, norm, bias
    return p


def projection_phase(nc, g, name, x_rows, x_sample, shift_block, scale_block, plan, loads=(), gate=None):
    D, K, T, NT, NS, NC = g.D, g.K, g.T, g.NT, g.NS, g.NS + 1
    HD = g.HD
    UB = NT + 1
    ROUNDS = NT // LINES
    NG = T // NB
    n = chain = helped_n = 0
    for p in plan:
        p.base, p.chain0, p.help0 = n, chain, helped_n
        p.chain_per = {"headnorm": 3, "logf": 4}.get(p.kind, 0)
        p.help_per = {"silu": 1, "headnorm": 2, "logf": 1}.get(p.kind, 0)
        n, chain, helped_n = n + p.blocks, chain + p.chain_per * UB * p.blocks, helped_n + p.help_per * UB * p.blocks
    n_blocks = n
    with ExitStack() as st:
        sb = lambda n, s, d=F32: st.enter_context(nc.sbuf_tensor(f"{name}_{n}", s, d))
        sem = lambda n: g.sem(f"{name}_{n}")
        h_hi, h_lo = sb("h_hi", [P, K, T], F32R), sb("h_lo", [P, K, T], F32R)
        hs_hi, hs_lo = sb("hs_hi", [P, K, P], F32R), sb("hs_lo", [P, K, P], F32R)
        w_hi, w_lo = sb("w_hi", [P, K, NB], F32R), sb("w_lo", [P, K, NB], F32R)
        w_raw = sb("w_raw", [P, K, NB])
        aux = sb("aux", [P, max(LINES * NB, T)])
        stage = sb("stage", [P, LINES * NB])
        stage_s = sb("stage_s", [P, NB])
        small = sb("small", [P, 64])
        x_in = [aux[:, u * D:(u + 1) * D] for u in range(2)]
        x_in += [w_raw[:, 2 * u:2 * u + 2, :].rearrange("p a b -> p (a b)") for u in range(2)]
        f_tile = [stage[:, u * D:(u + 1) * D] for u in range(2)]
        modT = g.modT[:, :].rearrange("p (b c) -> p b c", c=NC)
        sum_sq, r_x = small[:, 0:XS], small[:, XS:2 * XS]

        x_loaded = [sem(f"x_loaded{u}") for u in range(XS)]
        x_turned, f_ready, lo_done, hi_done = sem("x_turned"), sem("f_ready"), sem("h_lo_done"), sem("h_hi_done")
        norm_chain, r_ready, r_x_ready, xn_ready = sem("norm_chain"), sem("r_ready"), sem("r_x_ready"), sem("xn_ready")
        pads_clear, fs_chain = sem("pads_clear"), sem("fs_chain")
        w_loaded, w_hi_done, w_ready, w_free = sem("w_loaded"), sem("w_hi_done"), sem("w_ready"), sem("w_free")
        ps_full, evac_done = sem("ps_full"), sem("evac_done")
        helped, help_chain, dve_chain = sem("act_helped"), sem("act_help_chain"), sem("dve_chain")
        loads_done, loads_fixed = sem("loads_done"), sem("loads_fixed")
        stored = [sem(f"stored{s}") for s in range(LINES + 1)]
        if gate:
            z_cols = gate.w2.shape[0]
            w2 = w_raw[0:z_cols, 5, 0:g.HA * g.DK]
            z_raw = w_raw[:, 7, 0:K * z_cols].rearrange("p (k n) -> p k n", n=z_cols)
            zT, zs = aux[0:z_cols, 0:T], stage_s[0:z_cols, 0:NS]
            x_tmp = [w_raw[:, u, :] for u in range(2)]
            abs_tmp = [w_raw[:, 2 + u, :] for u in range(2)]
            in_chunk = w_raw[:, 4, :]
            pieces = g.HA * NG
            z_pads, z_full, z_ready, pre_full = sem("z_pads"), sem("z_full"), sem("z_ready"), sem("pre_full")
            pre_chain, gate_helped, gate_chain = sem("pre_chain"), sem("gate_helped"), sem("gate_chain")
            gate_act_chain, gate_done, mask_made = sem("gate_act_chain"), sem("gate_done"), sem("mask_made")
        ps_x = [[g.bank[2 * u + b][:, :].rearrange("p (k c) -> p k c", c=P) for b in range(2)] for u in range(2)]

        def gate_loads(sp):
            sp.wait_ge(w_ready, K * n_blocks + K)
            c0 = gate.first * NB
            sp.dma_start(w2, gate.w2).then_inc(w_loaded, 16)
            sp.dma_start(z_raw, gate.w.rearrange("(k p) n -> p k n", p=P)[:, :, c0:c0 + z_cols])\
                .then_inc(w_loaded, 16)
            for i in range(pieces):
                sp.wait_ge(gate_done, i + 1)
                sp.dma_start(gate.out[i // NG * P:(i // NG + 1) * P, i % NG * NB:(i % NG + 1) * NB],
                             stage[:, i % LINES * NB:(i % LINES + 1) * NB]).then_inc(stored[i % LINES], 16)
            sp.wait_ge(gate_done, pieces + 1)
            sp.dma_start(gate.out_s, stage_s[:, 0:g.HA * NS]).then_inc(stored[LINES], 16)

        def gate_products(pe, three_passes):
            pe.wait_ge(evac_done, UB * n_blocks + LINES)
            pe.wait_ge(w_ready, K * n_blocks + K + K)
            pe.wait_ge(z_pads, 2)
            for q in range(NG + 1):
                out = g.bank[q][:, :] if q < NG else g.bank[LINES][:, 0:NS]
                for k in range(K):
                    h_part = ((h_hi[:, k, q * NB:(q + 1) * NB], h_lo[:, k, q * NB:(q + 1) * NB]) if q < NG else
                              (hs_hi[:, k, 0:NS], hs_lo[:, k, 0:NS]))
                    mm = three_passes(out, (w_hi[:, k, 0:P], w_lo[:, k, 0:P]), h_part, k == 0, k == K - 1)
                mm.then_inc(z_full, 1)
            pe.wait_ge(z_ready, NG + 1)
            for i in range(pieces):
                if i >= LINES:
                    pe.wait_ge(gate_done, i - LINES + 1)
                pe.matmul(g.bank[i % LINES][:, :], w2[:, i // NG * P:(i // NG + 1) * P],
                          zT[:, i % NG * NB:(i % NG + 1) * NB], start=True, stop=True).then_inc(pre_full, 1)
            for hh in range(g.HA):
                mm = pe.matmul(g.bank[LINES][:, hh * NS:(hh + 1) * NS], w2[:, hh * P:(hh + 1) * P], zs,
                               start=True, stop=True)
            mm.then_inc(pre_full, 1)

        def gate_help(act):
            act.wait_ge(w_loaded, 16 * n_blocks + 32)
            for k in range(K):
                act.wait_ge(w_free, K * n_blocks + k + 1)
                act.activation(w_hi[:, k, 0:z_cols], z_raw[:, k, :], ACT.Copy).then_inc(w_hi_done, 1)
            for i in range(pieces + 1):
                a = abs_tmp[i % 2] if i < pieces else abs_tmp[i % 2][:, 0:g.HA * NS]
                act.wait_ge(pre_chain, i + 1)
                act.activation(a, a, ACT.Exp, scale=-1.0).then_inc(gate_act_chain, 1)
                act.wait_ge(gate_act_chain, i + 1)
                act.activation(a, a, ACT.Ln, bias=g.one[:, :]).then_inc(gate_helped, 1)

        def gate_elementwise(dve):
            dve.wait_ge(w_free, K * n_blocks + K)
            for part in (w_hi, w_lo):
                dve.memset(part[:, :, z_cols:P].bitcast(F32), 0.0).then_inc(z_pads, 1)
            for k in range(K):
                dve.wait_ge(w_hi_done, K * n_blocks + k + 1)
                dve.tensor_tensor(w_lo[:, k, 0:z_cols], z_raw[:, k, :], w_hi[:, k, 0:z_cols].bitcast(F32),
                                  ALU.subtract).then_inc(w_ready, 1)
            dve.wait_ge(w_ready, K * n_blocks + K + K)
            dve.memset(in_chunk, 1.0).then_inc(mask_made, 1)
            dve.wait_ge(mask_made, 1)
            dve.memset(in_chunk[:, 0:NB:P], 0.0).then_inc(mask_made, 1)
            dve.wait_ge(stored[LINES], 16 * n_blocks + 16)
            for q in range(NG + 1):
                dve.wait_ge(z_full, q + 1)
                if q < NG:
                    dve.tensor_copy(zT[:, q * NB:(q + 1) * NB], g.bank[q][0:z_cols, :]).then_inc(z_ready, 1)
                else:
                    dve.tensor_copy(zs, g.bank[LINES][0:z_cols, 0:NS]).then_inc(z_ready, 1)

            def begin(i):
                dve.wait_ge(pre_full, i + 1)
                if i >= 2:
                    dve.wait_ge(gate_done, i - 1)
                if i < pieces:
                    x, a = x_tmp[i % 2], abs_tmp[i % 2]
                    op = dve.tensor_scalar(x, g.bank[i % LINES][:, :], gate.bias[:, i // NG:i // NG + 1], None, ALU.add)
                else:
                    x, a = x_tmp[i % 2][:, 0:g.HA * NS], abs_tmp[i % 2][:, 0:g.HA * NS]
                    op = dve.tensor_tensor(x.rearrange("p (h s) -> p h s", s=NS),
                                           g.bank[LINES][:, 0:g.HA * NS].rearrange("p (h s) -> p h s", s=NS),
                                           gate.bias[:, :].unsqueeze(2).broadcast_to([P, g.HA, NS]), ALU.add)
                op.then_inc(gate_chain, 1)
                dve.wait_ge(gate_chain, 3 * i - 1 if i else 1)
                dve.scalar_tensor_tensor(a, x, -1.0, x, ALU.mult, ALU.max).then_inc(pre_chain, 1)

            def finish(i):
                w = NB if i < pieces else g.HA * NS
                x, a = x_tmp[i % 2][:, 0:w], abs_tmp[i % 2][:, 0:w]
                before = 3 * i + 2 if i < pieces else 3 * i + 1
                dve.wait_ge(gate_helped, i + 1)
                dve.scalar_tensor_tensor(x, x, 0.0, a, ALU.min, ALU.subtract).then_inc(gate_chain, 1)
                dve.wait_ge(gate_chain, before + 1)
                if i < pieces:
                    dve.tensor_scalar(x, x, 1.0 / GATE_TAU, None, ALU.mult).then_inc(gate_chain, 1)
                    dve.wait_ge(gate_chain, before + 2)
                    rounds = ROUNDS * n_blocks + i // LINES
                    dve.wait_ge(stored[i % LINES], 16 * rounds + 16)
                    dve.tensor_tensor_scan(stage[:, i % LINES * NB:(i % LINES + 1) * NB], in_chunk, x, 0.0,
                                           ALU.mult, ALU.add).then_inc(gate_done, 1)
                else:
                    dve.tensor_scalar(stage_s[:, 0:w], x, 1.0 / GATE_TAU, None, ALU.mult).then_inc(gate_done, 1)
            begin(0)
            for i in range(pieces):
                begin(i + 1)
                finish(i)
            finish(pieces)

        with nc.Block() as block:
            @block.sync
            def _(sp):
                def load_x(h, u, sample=False):
                    sp.wait_ge(x_turned, XS * h + u + 1)
                    if sample:
                        sp.dma_start(x_in[u][0:NS, :], x_sample).then_inc(x_loaded[u], 16)
                    else:
                        sp.dma_start(x_in[u], x_rows[ds((XS * h + u) * P, P), :]).then_inc(x_loaded[u], 16)

                def load_w(p, j):
                    sp.wait_ge(w_ready, K * (p.base + j) + K)
                    src = (col_blocks(p.w, p.first + j) if p.width == NB else
                           p.w.rearrange("(k p) n -> p k n", p=P)[:, :, p.first * NB:p.first * NB + p.width])
                    sp.dma_start(w_raw[:, :, 0:p.width], src).then_inc(w_loaded, 16)

                def store_units(p, j):
                    for t in range(NT):
                        sp.wait_ge(evac_done, UB * (p.base + j) + t + 1 + LINES)
                        dst = (p.out[ds(j * NB + t // NG * P, P), t % NG * NB:(t % NG + 1) * NB]
                               if p.kind == "transposed" else p.out[t * P:(t + 1) * P, ds(j * p.width, p.width)])
                        s = t % LINES
                        sp.dma_start(dst, stage[:, s * NB:s * NB + p.width]).then_inc(stored[s], 16)
                    sp.wait_ge(evac_done, UB * (p.base + j) + UB + LINES)
                    if p.kind == "transposed":
                        c = NB // P * NS
                        sp.dma_start(p.out_s[:, ds(j * c, c)], stage_s[:, 0:c]).then_inc(stored[LINES], 16)
                    else:
                        sp.dma_start(p.out_s[:, ds(j * p.width, p.width)], stage_s[0:NS, 0:p.width])\
                            .then_inc(stored[LINES], 16)

                for dst, src in loads:
                    sp.dma_start(dst, src).then_inc(loads_done, 16)
                with sp.Fori(0, NT // XS) as h:
                    for u in range(XS):
                        load_x(h, u)
                load_x(NT // XS, 0, True)
                sp.wait_ge(x_turned, NT + XS)
                load_w(plan[0], 0)
                block_groups(sp, plan, lambda p, j: None, load_w, store_units)
                if gate:
                    gate_loads(sp)
                for s in range(LINES):
                    sp.wait_ge(stored[s], 16 * (ROUNDS * n_blocks + (pieces // LINES if gate else 0) + 1))
                sp.wait_ge(stored[LINES], 16 * (n_blocks + (1 if gate else 0) + 1))

            @block.tensor
            def _(pe):
                def turn_x(h, u, *_, rows=P):
                    pe.wait_ge(xn_ready, XS * h + u + 1)
                    pe.wait_ge(f_ready, XS * h + u + 1)
                    for k in range(K):
                        mm = pe.transpose(ps_x[u % 2][k // 4][:, k % 4, 0:rows], x_in[u][0:rows, k * P:(k + 1) * P],
                                          g.ident[0:rows, 0:rows])
                    mm.then_inc(x_turned, 1)

                def three_passes(out, left, right, first, last):
                    pe.matmul(out, left[0], right[0], start=first, stop=False)
                    pe.matmul(out, left[0], right[1], start=False, stop=False)
                    return pe.matmul(out, left[1], right[0], start=False, stop=last)

                def block_units(p, j):
                    n = p.base + j
                    for t in range(NT):
                        pe.wait_ge(evac_done, UB * n + t + 1)
                        out = g.bank[t % LINES][:, 0:p.width]
                        for k in range(K):
                            if t == 0:
                                pe.wait_ge(w_ready, K * n + k + 1 + K)
                            w_cols = slice(t // NG * P, t // NG * P + P) if p.kind == "transposed" else slice(0, p.width)
                            h_cols = (slice(t % NG * NB, (t % NG + 1) * NB) if p.kind == "transposed" else
                                      slice(t * P, (t + 1) * P))
                            w_part = (w_hi[:, k, w_cols], w_lo[:, k, w_cols])
                            h_part = (h_hi[:, k, h_cols], h_lo[:, k, h_cols])
                            left, right = (w_part, h_part) if p.kind == "transposed" else (h_part, w_part)
                            mm = three_passes(out, left, right, k == 0, k == K - 1)
                        mm.then_inc(ps_full, 1)
                    pe.wait_ge(evac_done, UB * n + NT + 1)
                    if p.kind == "transposed":
                        for m in range(NB // P):
                            for k in range(K):
                                w_part = (w_hi[:, k, m * P:(m + 1) * P], w_lo[:, k, m * P:(m + 1) * P])
                                mm = three_passes(g.bank[LINES][:, m * NS:(m + 1) * NS], w_part,
                                                  (hs_hi[:, k, 0:NS], hs_lo[:, k, 0:NS]), k == 0, k == K - 1)
                                if m == NB // P - 1:
                                    mm.then_inc(w_free, 1)
                    else:
                        for k in range(K):
                            w_part = (w_hi[:, k, 0:p.width], w_lo[:, k, 0:p.width])
                            three_passes(g.bank[LINES][:, 0:p.width], (hs_hi[:, k, :], hs_lo[:, k, :]), w_part,
                                         k == 0, k == K - 1).then_inc(w_free, 1)

                pe.sem_inc(x_turned, XS)
                pe.sem_inc(w_free, K)
                with pe.Fori(0, NT // XS) as h:
                    for u in range(XS):
                        turn_x(h, u)
                turn_x(NT // XS, 0, rows=NS)
                pe.wait_ge(hi_done, NT + 1)
                pe.wait_ge(lo_done, NT + 1 + 2)
                for p in plan:
                    with pe.Fori(0, p.blocks) as j:
                        block_units(p, j)
                if gate:
                    gate_products(pe, three_passes)

            @block.scalar
            def _(act):
                def norm_scale(h, u, rows=P):
                    t = XS * h + u
                    act.wait_ge(x_loaded[u], 16 * h + 16)
                    act.activation(w_lo[0:rows, 2 * u:2 * u + 2, :],
                                   x_in[u][0:rows].rearrange("p (a b) -> p a b", b=NB), ACT.Square,
                                   scale=float(D) ** -0.5, accum_out=sum_sq[0:rows, u:u + 1]).then_inc(norm_chain, 1)
                    act.wait_ge(norm_chain, t + 1)
                    act.activation(sum_sq[0:rows, u:u + 1], sum_sq[0:rows, u:u + 1], ACT.Sqrt,
                                   bias=g.eps[0:rows, :]).then_inc(r_ready, 1)

                def high(h, u):
                    t = XS * h + u
                    act.wait_ge(f_ready, t + 1 + 2)
                    act.activation(h_hi[:, :, ds(t * P, P)], f_tile[u % 2].rearrange("p (k c) -> p k c", c=P),
                                   ACT.Copy).then_inc(hi_done, 1)

                def high_sample(h, u):
                    act.wait_ge(f_ready, NT + 1 + 2)
                    act.wait_ge(pads_clear, 2)
                    act.activation(hs_hi[:, :, 0:NS], f_tile[u][:, 0:K * NS].rearrange("p (k c) -> p k c", c=NS),
                                   ACT.Copy).then_inc(hi_done, 1)

                def split_high(p, j):
                    n = p.base + j
                    act.wait_ge(w_loaded, 16 * n + 16)
                    for k in range(K):
                        act.wait_ge(w_free, K * n + k + 1)
                        act.activation(w_hi[:, k, 0:p.width], w_raw[:, k, 0:p.width], ACT.Copy).then_inc(w_hi_done, 1)

                def help_unit(p, j, t):
                    n = p.base + j
                    rows = NS if t == NT else P
                    u = t % 2
                    ps = g.bank[t % LINES if t < NT else LINES][0:rows, 0:p.width]
                    tmp = aux[0:rows, u * NB:(u + 1) * NB]
                    c = p.chain0 + p.chain_per * (UB * j + t)
                    hn = UB * n + t
                    if p.kind in ("silu", "headnorm"):
                        if t < NT:
                            act.wait_ge(ps_full, NT * n + t + 1)
                        else:
                            act.wait_ge(w_free, K * n + K + K)
                        act.wait_ge(evac_done, hn - 1 + (t == 0) + LINES)
                    if p.kind == "silu":
                        act.activation(tmp, ps, ACT.Silu).then_inc(helped, 1)
                    if p.kind == "headnorm":
                        act.activation(tmp, ps, ACT.Square, scale=float(HD) ** -0.5).then_inc(helped, 1)
                        ms = small[0:rows, 8 + 16 * u:16 + 16 * u]
                        act.wait_ge(dve_chain, c + 1)
                        act.activation(ms, ms, ACT.Sqrt, bias=g.eps[0:rows, :]).then_inc(helped, 1)
                    if p.kind == "logf":
                        a = tmp[:, 16:32]
                        act.wait_ge(dve_chain, c + 2)
                        act.activation(a, a, ACT.Exp, scale=-1.0).then_inc(help_chain, 1)
                        act.wait_ge(help_chain, UB * j + t + 1 + p.act0)
                        act.activation(a, a, ACT.Ln, bias=g.one[0:rows, :]).then_inc(helped, 1)

                act0 = 0
                for p in plan:
                    p.act0 = act0
                    act0 += UB * p.blocks if p.kind == "logf" else 0
                norm_scale(0, 0)
                norm_scale(0, 1)
                looped = (NT - 2) // XS
                with act.Fori(0, looped) as h:
                    for u in range(XS):
                        norm_scale(h + (u + 2) // XS, (u + 2) % XS)
                        high(h, u)
                for t in range(XS * looped, NT):
                    if t + 2 < NT:
                        norm_scale((t + 2) // XS, (t + 2) % XS)
                    if t + 2 == NT:
                        norm_scale(NT // XS, 0, NS)
                    high(t // XS, t % XS)
                high_sample(NT // XS, 0)
                split_high(plan[0], 0)
                block_groups(act, plan, lambda p, j: [help_unit(p, j, t) for t in range(NT - 1)], split_high,
                             lambda p, j: [help_unit(p, j, t) for t in (NT - 1, NT)])
                if gate:
                    gate_help(act)

            @block.vector
            def _(dve):
                def scale_x(h, u, rows=P):
                    dve.wait_ge(r_ready, XS * h + u + 1)
                    dve.reciprocal(r_x[0:rows, u:u + 1], sum_sq[0:rows, u:u + 1]).then_inc(r_x_ready, 1)
                    dve.wait_ge(r_x_ready, XS * h + u + 1)
                    dve.tensor_scalar(x_in[u][0:rows], x_in[u][0:rows], r_x[0:rows, u:u + 1], None,
                                      ALU.mult).then_inc(xn_ready, 1)

                def modulate(h, u):
                    dve.wait_ge(x_turned, XS * h + u + 1 + XS)
                    dve.wait_ge(lo_done, XS * h + u + 1)
                    for k in range(K):
                        op = dve.tensor_scalar(f_tile[u % 2][:, k * P:(k + 1) * P], ps_x[u % 2][k // 4][:, k % 4, :],
                                               modT[:, scale_block + k, 0:1], modT[:, shift_block + k, 0:1],
                                               ALU.mult, ALU.add)
                    op.then_inc(f_ready, 1)

                def modulate_sample(h, u):
                    dve.wait_ge(x_turned, NT + 1 + XS)
                    dve.wait_ge(lo_done, NT + 1)
                    f = f_tile[u][:, 0:K * NS].rearrange("p (k c) -> p k c", c=NS)
                    for b in range(2):
                        dve.tensor_tensor(f[:, 4 * b:4 * b + 4, :], ps_x[u][b][:, :, 0:NS],
                                          modT[:, scale_block + 4 * b:scale_block + 4 * b + 4, 1:NC],
                                          ALU.mult).then_inc(fs_chain, 1)
                    dve.wait_ge(fs_chain, 2)
                    dve.tensor_tensor(f, f, modT[:, shift_block:shift_block + K, 1:NC], ALU.add).then_inc(f_ready, 1)

                def split_low(p, j):
                    n = p.base + j
                    for k in range(K):
                        dve.wait_ge(w_hi_done, K * n + k + 1)
                        dve.tensor_tensor(w_lo[:, k, 0:p.width], w_raw[:, k, 0:p.width],
                                          w_hi[:, k, 0:p.width].bitcast(F32), ALU.subtract).then_inc(w_ready, 1)

                def evacuate(p, j, t):
                    n = p.base + j
                    rows = NS if t == NT else P
                    u, s = t % 2, (t % LINES if t < NT else LINES)
                    ps = g.bank[s][0:rows, 0:p.width]
                    tmp = aux[0:rows, u * NB:(u + 1) * NB]
                    out = stage[0:rows, s * NB:s * NB + p.width] if t < NT else stage_s[0:rows, 0:p.width]
                    c = p.chain0 + p.chain_per * (UB * j + t)
                    hn = p.help0 + p.help_per * (UB * j + t)
                    if p.kind == "transposed" and t == NT:
                        ps, out = g.bank[s][:, 0:NB // P * NS], stage_s[:, 0:NB // P * NS]
                    if t < NT:
                        dve.wait_ge(ps_full, NT * n + t + 1)
                        dve.wait_ge(stored[s], 16 * (ROUNDS * n + t // LINES) + 16)
                    else:
                        dve.wait_ge(w_free, K * n + K + K)
                        dve.wait_ge(stored[s], 16 * n + 16)
                    if p.kind in ("plain", "transposed"):
                        if p.scale is None:
                            dve.tensor_copy(out, ps).then_inc(evac_done, 1)
                        else:
                            dve.tensor_scalar(out, ps, p.scale, None, ALU.mult).then_inc(evac_done, 1)
                    if p.kind == "silu":
                        dve.wait_ge(helped, hn + 1)
                        dve.tensor_copy(out, tmp).then_inc(evac_done, 1)
                    if p.kind == "headnorm":
                        heads = NB // HD
                        ms = small[0:rows, 8 + 16 * u:16 + 16 * u]
                        r = small[0:rows, 16 + 16 * u:24 + 16 * u]
                        split = lambda a: a.rearrange("p (h d) -> p h d", d=HD)
                        dve.wait_ge(helped, hn + 1)
                        dve.tensor_reduce(ms, split(tmp), AX.X, ALU.add).then_inc(dve_chain, 1)
                        dve.wait_ge(helped, hn + 2)
                        dve.reciprocal(r, ms).then_inc(dve_chain, 1)
                        dve.wait_ge(dve_chain, c + 2)
                        dve.tensor_tensor(split(out), split(ps), r.unsqueeze(2).broadcast_to([rows, heads, HD]),
                                          ALU.mult).then_inc(dve_chain, 1)
                        dve.wait_ge(dve_chain, c + 3)
                        dve.tensor_tensor(split(out), split(out),
                                          p.norm[0:rows, :].unsqueeze(1).broadcast_to([rows, heads, HD]),
                                          ALU.mult).then_inc(evac_done, 1)
                    if p.kind == "logf":
                        x, a = tmp[:, 0:16], tmp[:, 16:32]
                        dve.tensor_tensor(x, ps, p.bias[0:rows, :], ALU.add).then_inc(dve_chain, 1)
                        dve.wait_ge(dve_chain, c + 1)
                        dve.scalar_tensor_tensor(a, x, -1.0, x, ALU.mult, ALU.max).then_inc(dve_chain, 1)
                        dve.wait_ge(helped, hn + 1)
                        dve.scalar_tensor_tensor(out, x, 0.0, a, ALU.min, ALU.subtract).then_inc(dve_chain, 1)
                        dve.wait_ge(dve_chain, c + 3)
                        keep = g.logf_all[0:rows, t * 16:(t + 1) * 16] if t < NT else g.logf_s[0:rows, :]
                        dve.tensor_copy(keep, out).then_inc(dve_chain, 1)
                        dve.wait_ge(dve_chain, c + 4)
                        dve.sem_inc(evac_done, 1)

                dve.sem_inc(f_ready, 2)
                dve.sem_inc(w_ready, K)
                dve.sem_inc(evac_done, LINES)
                for s in range(LINES + 1):
                    dve.sem_inc(stored[s], 16)
                for pad in (hs_hi, hs_lo):
                    dve.memset(pad[:, :, :].bitcast(F32), 0.0).then_inc(pads_clear, 1)
                in_turn(dve, NT, scale_x, lambda h, u, h1, u1: (scale_x(h1, u1), modulate(h, u)),
                        lambda h, u: (scale_x(NT // XS, 0, NS), modulate(h, u), modulate_sample(NT // XS, 0)))
                dve.wait_ge(loads_done, 16 * len(loads)) if loads else None
                for p in plan:
                    if p.kind == "headnorm" and p.scale is not None:
                        dve.tensor_scalar(p.norm, p.norm, p.scale, None, ALU.mult).then_inc(loads_fixed, 1)
                        dve.wait_ge(loads_fixed, 1)
                split_low(plan[0], 0)
                block_groups(dve, plan, lambda p, j: [evacuate(p, j, t) for t in range(NT - 1)], split_low,
                             lambda p, j: [evacuate(p, j, t) for t in (NT - 1, NT)])
                if gate:
                    gate_elementwise(dve)

            @block.gpsimd
            def _(pool):
                def low(h, u):
                    t = XS * h + u
                    pool.wait_ge(hi_done, t + 1)
                    pool.tensor_tensor(h_lo[:, :, ds(t * P, P)], f_tile[u % 2].rearrange("p (k c) -> p k c", c=P),
                                       h_hi[:, :, ds(t * P, P)].bitcast(F32), ALU.subtract).then_inc(lo_done, 1)

                pool.sem_inc(lo_done, 2)
                with pool.Fori(0, NT // XS) as h:
                    for u in range(XS):
                        low(h, u)
                pool.wait_ge(hi_done, NT + 1)
                pool.tensor_tensor(hs_lo[:, :, 0:NS], f_tile[0][:, 0:K * NS].rearrange("p (k c) -> p k c", c=NS),
                                   hs_hi[:, :, 0:NS].bitcast(F32), ALU.subtract).then_inc(lo_done, 1)


def gla_projections(nc, g):
    w = g.i.gla_w_in[0]
    with ExitStack() as st:
        b_g = st.enter_context(nc.sbuf_tensor("b_g", [P, g.HA], F32))
        loads = []
        for hh in range(g.HA):
            loads.append((b_g[:, hh:hh + 1], g.i.gla_b_g[0:1, hh * P:(hh + 1) * P].rearrange("a p -> p a")))
        plan = [group("transposed", w, 0, 1, g.qT, g.qT_s, scale=float(g.DK) ** -0.5),
                group("transposed", w, 1, 1, g.kT, g.kT_s),
                group("plain", w, 2, 2, g.v_gla, g.v_gla_s),
                group("silu", w, 4, 2, g.sg_gla, g.sg_gla_s)]
        gate = Names()
        gate.w, gate.first, gate.w2, gate.bias = w, 6, g.i.gla_w_g2[0], b_g
        gate.out, gate.out_s = g.bT, g.aT_s
        projection_phase(nc, g, "gla", g.i.x_prompt[0], g.i.x_sample[:, 0, :], g.mod_gla, g.mod_gla + g.K,
                         plan, loads, gate)


def split_output_weight(act, dve, w_raw, w_hi, w_lo, w_loaded, hi_done, ready, K, row_scale=None, scaled=None):
    if act is not None:
        for k in range(K):
            if row_scale is not None:
                act.wait_ge(scaled, k + 1)
            elif k == 0:
                act.wait_ge(w_loaded, 16)
            act.activation(w_hi[:, k, :], w_raw[:, k, :], ACT.Copy).then_inc(hi_done, 1)
    if dve is not None:
        if row_scale is not None:
            dve.wait_ge(w_loaded, 16)
            for k in range(K):
                dve.tensor_scalar(w_raw[:, k, :], w_raw[:, k, :], row_scale[k], None, ALU.mult).then_inc(scaled, 1)
        for k in range(K):
            dve.wait_ge(hi_done, k + 1)
            dve.tensor_tensor(w_lo[:, k, :], w_raw[:, k, :], w_hi[:, k, :].bitcast(F32), ALU.subtract)\
               .then_inc(ready, 1)


def gla_phase(nc, g):
    D, K, NT, NS, HA, DV = g.D, g.K, g.NT, g.NS, g.HA, g.DV
    Q4, HALF = P // 4, P // 2
    NC = NS + 1
    with ExitStack() as st:
        sb = lambda n, s, d=F32: st.enter_context(nc.sbuf_tensor(f"gl_{n}", s, d))
        sem = lambda n: g.sem(f"gl_{n}")
        w_raw = sb("w_raw", [P, K, D])
        w_hi, w_lo = sb("w_hi", [P, K, D], F32R), sb("w_lo", [P, K, D], F32R)
        onorm = sb("onorm", [P, DV // P])
        gate = sb("gate", [P, D])
        q, k, b = (sb(n, [P, HA, P]) for n in "qkb")
        v, sg, x = (sb(n, [P, HA * DV]) for n in ("v", "sg", "x"))
        d_own, d_near, d_far, d_end = (sb(n, [P, HA, P]) for n in ("d_own", "d_near", "d_far", "d_end"))
        e_own_q, e_own_k, e_near, e_far = (sb(n, [P, HA, P]) for n in ("e_own_q", "e_own_k", "e_near", "e_far"))
        e_start, e_end = sb("e_start", [P, HA, P]), sb("e_end", [P, HA, P])
        decay = sb("decay", [P, HA])
        q_own, k_own, qk_near = sb("q_own", [P, HA, P]), sb("k_own", [P, HA, P]), sb("qk_near", [P, HA, P])
        q_far, k_far = sb("q_far", [P, HA, P]), sb("k_far", [P, HA, P])
        q_state, k_state = sb("q_state", [P, HA, P]), sb("k_state", [P, HA, P])
        k_rows, att = sb("k_rows", [P, HA, P]), sb("att", [P, HA, P])
        S = sb("S", [P, HA, DV])
        squares, og = sb("squares", [P, HA, DV]), sb("og", [P, HA * DV])
        stats, ln_ms, r_o = sb("stats", [P, HA]), sb("ln_ms", [P, HA]), sb("r_o", [P, HA])
        oT_hi, oT_lo = sb("oT_hi", [P, K, P], F32R), sb("oT_lo", [P, K, P], F32R)
        y = sb("y", [P, D])
        qs, ks, as_ = (sb(n, [P, HA * NS]) for n in ("qs", "ks", "as"))
        q_one = sb("q_one", [P, HA, NS * NS])
        s_in = [w_raw[:, u, :].rearrange("p (h d) -> p h d", d=DV) for u in range(2)]
        s_out = [w_raw[:, 2 + u, :].rearrange("p (h d) -> p h d", d=DV) for u in range(2)]
        v_all = [w_raw[:, 4 + u, :] for u in range(2)]
        sg_s, x_s, gate_s, og_s, y_s = (sb(n, [NS, D]) for n in ("sg_s", "x_s", "gate_s", "og_s", "y_s"))

        w_loaded, w_scaled, w_hi_done, w_ready = sem("w_loaded"), sem("w_scaled"), sem("w_hi_done"), sem("w_ready")
        gate_loaded, cleared = sem("gate_loaded"), sem("cleared")
        qkb_loaded, v_loaded, sg_loaded, x_loaded = (sem(f"{n}_loaded") for n in ("qkb", "v", "sg", "x"))
        diff_chain, diff_done, exp_done = sem("diff_chain"), sem("diff_done"), sem("exp_done")
        att_in_ready, prep_done = sem("att_in_ready"), sem("prep_done")
        att_full, att_ready, kT_full, k_rows_ready = sem("att_full"), sem("att_ready"), sem("kT_full"), sem("k_rows_ready")
        o_full, kv_full, s_ready = sem("o_full"), sem("kv_full"), sem("s_ready")
        stat_chain, r_ready, og_done = sem("stat_chain"), sem("r_ready"), sem("og_done")
        oT_full, oT_hi_done, oT_lo_done = sem("oT_full"), sem("oT_hi_done"), sem("oT_lo_done")
        y_full, y_chain, y_done, x1_stored = sem("y_full"), sem("y_chain"), sem("y_done"), sem("x1_stored")
        state_stored, small_loaded = sem("state_stored"), sem("small_loaded")
        s_loaded = [sem(f"s_loaded{u}") for u in range(2)]
        v_all_loaded = [sem(f"v_all_loaded{u}") for u in range(2)]
        s_stored = [sem(f"s_stored{u}") for u in range(2)]
        q_one_ready, a_ready, s_chain, s_made, s_used = (sem(n) for n in ("q_one_ready", "a_ready", "s_chain",
                                                                          "s_made", "s_used"))
        ps_att, ps_kT = g.bank[0], g.bank[1]
        ps_o = [g.bank[2 + hh // 2][:, hh % 2 * DV:(hh % 2 + 1) * DV] for hh in range(HA)]
        ps_kv = [g.bank[4 + hh // 2][:, hh % 2 * DV:(hh % 2 + 1) * DV] for hh in range(HA)]
        ps_oT = [g.bank[4 + a][:, :].rearrange("p (k c) -> p k c", c=P) for a in range(2)]
        ps_y = g.bank[6:8]

        def steps(eng, step):
            step(0, True, NT == 1)
            with eng.Fori(1, NT - 1) as c:
                step(c, False, False)
            step(NT - 1, False, True)

        with nc.Block() as block:
            @block.sync
            def _(sp):
                def load_qkb(c, first=False):
                    if not first:
                        sp.wait_ge(prep_done, c + 1)
                        sp.wait_ge(exp_done, 9 * c)
                    for tile, src in ((q, g.qT), (k, g.kT), (b, g.bT)):
                        sp.dma_start(tile[:, :, :], src.rearrange("(h p) t -> p h t", p=P)[:, :, ds(c * P, P)])\
                            .then_inc(qkb_loaded, 16)

                def load_sg(c):
                    sp.dma_start(sg[:, :], g.sg_gla[ds(c * P, P), :]).then_inc(sg_loaded, 16)

                def load_v(c):
                    sp.dma_start(v[:, :], g.v_gla[ds(c * P, P), :]).then_inc(v_loaded, 16)

                def store_x1(c):
                    sp.dma_start(g.x1[ds(c * P, P), :], y[:, :]).then_inc(x1_stored, 16)

                def step(c, first, last):
                    if not last:
                        load_qkb(c + 1)
                        sp.wait_ge(og_done, c + 1)
                        load_sg(c + 1)
                        sp.wait_ge(kv_full, c + 1)
                        load_v(c + 1)
                    if not first:
                        sp.wait_ge(y_done, c + 1)
                        store_x1(c - 1)
                    sp.dma_start(x[:, :], g.i.x_prompt[0, ds(c * P, P), :]).then_inc(x_loaded, 16)

                load_qkb(0, first=True)
                load_sg(0)
                load_v(0)
                sp.dma_start(w_raw[:, :, :], g.i.gla_w_out[0].rearrange("(k p) n -> p k n", p=P)).then_inc(w_loaded, 16)
                for j in range(DV // P):
                    sp.dma_start(onorm[:, j:j + 1], g.i.gla_onorm[0:1, j * P:(j + 1) * P].rearrange("a p -> p a"))\
                        .then_inc(small_loaded, 16)
                G0 = (g.mod_gla + 2 * K) * P
                sp.dma_start(gate[:, :], g.mods[0:1, G0:G0 + D].broadcast_to([P, D])).then_inc(gate_loaded, 16)
                steps(sp, step)
                sp.wait_ge(y_done, NT + 1)
                store_x1(NT - 1)
                sp.wait_ge(s_ready, NT + 1)
                sp.dma_start(g.o.state_prompt[0, 0].rearrange("h p d -> p h d"), S[:, :, :]).then_inc(state_stored, 16)
                for tile, src in ((qs, g.qT_s), (ks, g.kT_s), (as_, g.aT_s), (sg_s, g.sg_gla_s),
                                  (x_s, g.i.x_sample[:, 0, :]), (gate_s, g.mods[1:NC, G0:G0 + D])):
                    sp.dma_start(tile[:, :], src).then_inc(small_loaded, 16)
                def load_s(s):
                    u = s % 2
                    if s >= 2:
                        sp.wait_ge(s_made, s - 1)
                    sp.dma_start(s_in[u], g.i.state_gla[0, s].rearrange("h p d -> p h d")).then_inc(s_loaded[u], 16)
                    sp.dma_start(v_all[u], g.v_gla_s[s:s + 1, :].broadcast_to([P, HA * DV])).then_inc(v_all_loaded[u], 16)
                load_s(0)
                load_s(1)
                for s in range(NS):
                    sp.wait_ge(s_made, s + 1)
                    sp.dma_start(g.o.state_sample[0, s].rearrange("h p d -> p h d"), s_out[s % 2]).then_inc(s_stored[s % 2], 16)
                    if s + 2 < NS:
                        load_s(s + 2)
                sp.wait_ge(y_done, NT + 2)
                sp.dma_start(g.x1_s, y_s[:, :]).then_inc(x1_stored, 16)
                sp.wait_ge(x1_stored, 16 * (NT + 2))
                sp.wait_ge(state_stored, 16)
                for u in range(2):
                    sp.wait_ge(s_stored[u], 16 * NS // 2)

            @block.tensor
            def _(pe):
                def attend(c):
                    pe.wait_ge(att_in_ready, c + 1)
                    for hh in range(HA):
                        a = ps_att[:, hh * P:(hh + 1) * P]
                        pe.matmul(a, k_far[:, hh, :], q_far[:, hh, :], start=True, stop=False, skip_group_check=True)
                        for i in range(2):
                            lo = slice(2 * i * Q4, (2 * i + 1) * Q4)
                            hi = slice((2 * i + 1) * Q4, (2 * i + 2) * Q4)
                            pe.matmul(a[lo, hi], qk_near[:, hh, lo], qk_near[:, hh, hi], start=False, stop=False,
                                      skip_group_check=True)
                        for i in range(4):
                            own = slice(i * Q4, (i + 1) * Q4)
                            mm = pe.matmul(a[own, own], k_own[:, hh, own], q_own[:, hh, own], start=False,
                                           stop=(i == 3), skip_group_check=True)
                    mm.then_inc(att_full, 1)
                    pe.wait_ge(prep_done, c + 1 + 1)
                    for hh in range(HA):
                        mm = pe.transpose(ps_kT[:, hh * P:(hh + 1) * P], k_state[:, hh, :], g.ident[:, :])
                    mm.then_inc(kT_full, 1)

                def read_and_update(c, first):
                    pe.wait_ge(att_ready, c + 1)
                    pe.wait_ge(v_loaded, 16 * c + 16)
                    pe.wait_ge(s_ready, c + 1)
                    if not first:
                        pe.wait_ge(og_done, c)
                    for hh in range(HA):
                        pe.matmul(ps_o[hh], att[:, hh, :], v[:, hh * DV:(hh + 1) * DV], start=True, stop=False)
                        mm = pe.matmul(ps_o[hh], q_state[:, hh, :], S[:, hh, :], start=False, stop=True)
                    mm.then_inc(o_full, 1)
                    pe.wait_ge(k_rows_ready, c + 1)
                    if not first:
                        pe.wait_ge(oT_lo_done, 2 * c)
                    for hh in range(HA):
                        mm = pe.matmul(ps_kv[hh], k_rows[:, hh, :], v[:, hh * DV:(hh + 1) * DV], start=True, stop=True)
                    mm.then_inc(kv_full, 1)

                def project(c):
                    pe.wait_ge(oT_lo_done, 2 * c + 2)
                    pe.wait_ge(y_done, c + 1)
                    for a in range(2):
                        cols = slice(a * NB, (a + 1) * NB)
                        for kk in range(K):
                            pe.matmul(ps_y[a][:, :], oT_hi[:, kk, :], w_hi[:, kk, cols], start=(kk == 0), stop=False)
                            pe.matmul(ps_y[a][:, :], oT_hi[:, kk, :], w_lo[:, kk, cols], start=False, stop=False)
                            mm = pe.matmul(ps_y[a][:, :], oT_lo[:, kk, :], w_hi[:, kk, cols], start=False,
                                           stop=(kk == K - 1))
                    mm.then_inc(y_full, 1)

                def turn_o(c):
                    pe.wait_ge(og_done, c + 1)
                    pe.wait_ge(s_ready, c + 2)
                    for kk in range(K):
                        mm = pe.transpose(ps_oT[kk // 4][:, kk % 4, :], og[:, kk * P:(kk + 1) * P], g.ident[:, :])
                    mm.then_inc(oT_full, 1)

                def step(c, first, last):
                    read_and_update(c, first)
                    if not first:
                        project(c - 1)
                    if not last:
                        attend(c + 1)
                    turn_o(c)

                pe.sem_inc(prep_done, 1)
                pe.wait_ge(cleared, 3)
                attend(0)
                pe.wait_ge(w_ready, K)
                steps(pe, step)
                project(NT - 1)
                pe.wait_ge(q_one_ready, 2)
                for s in range(NS):
                    pe.wait_ge(s_made, s + 1)
                    for hh in range(HA):
                        mm = pe.matmul(ps_o[hh][0:NS, :], q_one[:, hh, s * NS:(s + 1) * NS], s_out[s % 2][:, hh, :],
                                       start=(s == 0 and hh % 2 == 0), stop=(s == NS - 1), skip_group_check=True)
                    mm.then_inc(s_used, 1)
                pe.wait_ge(og_done, NT + 1)
                for kk in range(K):
                    mm = pe.matmul(g.bank[4][:, kk * NS:(kk + 1) * NS], og_s[:, kk * P:(kk + 1) * P],
                                   g.ident[0:NS, 0:NS], start=True, stop=True)
                mm.then_inc(oT_full, 1)
                project(NT)

            @block.scalar
            def _(act):
                def exponentials(c):
                    act.wait_ge(prep_done, c + 1)
                    near, far = (t[:, :, :].rearrange("p h (n e) -> p (h n) e", e=w)
                                 for t, w in ((d_near, HALF), (d_far, P)))
                    en, ef = (t[:, :, :].rearrange("p h (n e) -> p (h n) e", e=w)
                              for t, w in ((e_near, HALF), (e_far, P)))
                    for out, src, sign, diff in (
                            (e_own_q[:, :, :], d_own[:, :, :], 1.0, 1), (e_own_k[:, :, :], d_own[:, :, :], -1.0, 1),
                            (en[:, :, 0:Q4], near[:, :, 0:Q4], -1.0, 2), (en[:, :, Q4:HALF], near[:, :, Q4:HALF], 1.0, 2),
                            (ef[:, :, 0:HALF], far[:, :, 0:HALF], -1.0, 3), (ef[:, :, HALF:P], far[:, :, HALF:P], 1.0, 3),
                            (e_start[:, :, :], b[:, :, :], 1.0, 3), (e_end[:, :, :], d_end[:, :, :], -1.0, 4),
                            (decay[:, :].unsqueeze(2), b[:, :, P - 1:P], 1.0, 4)):
                        act.wait_ge(diff_done, 4 * c + diff)
                        act.activation(out, src, ACT.Exp, scale=sign).then_inc(exp_done, 1)

                def turn_rows(c):
                    act.wait_ge(kT_full, c + 1)
                    act.activation(k_rows[:, :, :].rearrange("p h c -> p (h c)"), ps_kT[:, :], ACT.Copy)\
                       .then_inc(k_rows_ready, 1)

                def norm_scale(c, rows=P):
                    for hh in range(HA):
                        op = act.activation(squares[0:rows, hh, :], ps_o[hh][0:rows, :], ACT.Square,
                                            accum_out=stats[0:rows, hh:hh + 1])
                    op.then_inc(stat_chain, 1)
                    act.wait_ge(stat_chain, 2 * c + 1)
                    act.activation(ln_ms[0:rows, :], stats[0:rows, :], ACT.Ln, scale=1.0 / DV,
                                   bias=g.eps[0:rows, :]).then_inc(stat_chain, 1)
                    act.wait_ge(stat_chain, 2 * c + 2)
                    act.activation(r_o[0:rows, :], ln_ms[0:rows, :], ACT.Exp, scale=-0.5).then_inc(r_ready, 1)

                def high(c):
                    act.wait_ge(oT_full, c + 1)
                    for a in range(2):
                        act.activation(oT_hi[:, 4 * a:4 * a + 4, :], ps_oT[a], ACT.Copy).then_inc(oT_hi_done, 1)

                def step(c, first, last):
                    act.wait_ge(o_full, c + 1)
                    norm_scale(c)
                    if not last:
                        exponentials(c + 1)
                        turn_rows(c + 1)
                    high(c)

                exponentials(0)
                turn_rows(0)
                split_output_weight(act, None, w_raw, w_hi, w_lo, w_loaded, w_hi_done, w_ready, K,
                                    [None] * K, w_scaled)
                steps(act, step)
                act.wait_ge(small_loaded, 16 * (DV // P + 6))
                act.activation(as_[:, :], as_[:, :], ACT.Exp).then_inc(a_ready, 1)
                act.wait_ge(s_used, NS)
                norm_scale(NT, NS)
                act.wait_ge(oT_full, NT + 1)
                act.wait_ge(cleared, 5)
                act.activation(oT_hi[:, :, 0:NS], g.bank[4][:, 0:K * NS].rearrange("p (k c) -> p k c", c=NS),
                               ACT.Copy).then_inc(oT_hi_done, 2)

            @block.vector
            def _(dve):
                def prepare(c):
                    dve.wait_ge(qkb_loaded, 48 * c + 48)
                    cut = lambda t, w: t[:, :, :].rearrange("p h (n e) -> p (h n) e", e=w)

                    def difference(out, w, ref):
                        n = HA * P // w
                        return dve.tensor_tensor(cut(out, w), cut(b, w), cut(b, w)[:, :, ref:ref + 1].broadcast_to([P, n, w]),
                                                 ALU.subtract)
                    difference(d_own, Q4, Q4 // 2 - 1).then_inc(diff_chain, 1)
                    dve.wait_ge(diff_chain, c + 1)
                    dve.tensor_scalar(d_own[:, :, :], d_own[:, :, :], 80.0, -80.0, ALU.min, ALU.max).then_inc(diff_done, 1)
                    difference(d_near, HALF, Q4 - 1).then_inc(diff_done, 1)
                    difference(d_far, P, HALF - 1).then_inc(diff_done, 1)
                    difference(d_end, P, P - 1).then_inc(diff_done, 1)
                    first, second = slice(0, Q4), slice(Q4, HALF)
                    for n, (out, left, right) in enumerate((
                            (q_own[:, :, :], q[:, :, :], e_own_q[:, :, :]), (k_own[:, :, :], k[:, :, :], e_own_k[:, :, :]),
                            (cut(qk_near, HALF)[:, :, first], cut(k, HALF)[:, :, first], cut(e_near, HALF)[:, :, first]),
                            (cut(qk_near, HALF)[:, :, second], cut(q, HALF)[:, :, second], cut(e_near, HALF)[:, :, second]),
                            (k_far[:, :, 0:HALF], k[:, :, 0:HALF], e_far[:, :, 0:HALF]),
                            (q_far[:, :, HALF:P], q[:, :, HALF:P], e_far[:, :, HALF:P]),
                            (q_state[:, :, :], q[:, :, :], e_start[:, :, :]), (k_state[:, :, :], k[:, :, :], e_end[:, :, :]))):
                        dve.wait_ge(exp_done, 9 * c + n + 1)
                        op = dve.tensor_tensor(out, left, right, ALU.mult)
                        if n == 5:
                            op.then_inc(att_in_ready, 1)
                        if n == 7:
                            op.then_inc(prep_done, 1)

                def mask(c):
                    dve.wait_ge(att_full, c + 1)
                    dve.tensor_tensor(att[:, :, :], ps_att[:, :].rearrange("p (h c) -> p h c", c=P),
                                      g.keep_le[:, :].unsqueeze(1).broadcast_to([P, HA, P]), ALU.mult).then_inc(att_ready, 1)

                def update_state(c):
                    dve.wait_ge(kv_full, c + 1)
                    dve.wait_ge(exp_done, 9 * c + 9)
                    for hh in range(HA):
                        op = dve.scalar_tensor_tensor(S[:, hh, :], S[:, hh, :], decay[:, hh:hh + 1], ps_kv[hh],
                                                      ALU.mult, ALU.add)
                    op.then_inc(s_ready, 1)

                def gate_o(c, sg_tile, og_tile, rows=P):
                    dve.wait_ge(r_ready, c + 1)
                    for hh in range(HA):
                        cols = slice(hh * DV, (hh + 1) * DV)
                        op = dve.scalar_tensor_tensor(og_tile[0:rows, cols], ps_o[hh][0:rows, :], r_o[0:rows, hh:hh + 1],
                                                      sg_tile[0:rows, cols], ALU.mult, ALU.mult)
                    op.then_inc(og_done, 1)

                def low(c):
                    for a in range(2):
                        dve.wait_ge(oT_hi_done, 2 * c + a + 1)
                        dve.tensor_tensor(oT_lo[:, 4 * a:4 * a + 4, :], ps_oT[a], oT_hi[:, 4 * a:4 * a + 4, :].bitcast(F32),
                                          ALU.subtract).then_inc(oT_lo_done, 1)

                def finish(c, x_tile, gate_tile, y_tile, rows=P):
                    dve.wait_ge(y_full, c + 1)
                    dve.wait_ge(x1_stored, 16 * c + 16)
                    for a in range(2):
                        cols = slice(a * NB, (a + 1) * NB)
                        dve.tensor_tensor(y_tile[0:rows, cols], ps_y[a][0:rows, :], gate_tile[0:rows, cols], ALU.mult)\
                           .then_inc(y_chain, 1)
                    dve.wait_ge(y_chain, 2 * c + 2)
                    dve.tensor_tensor(y_tile[0:rows, :], y_tile[0:rows, :], x_tile[0:rows, :], ALU.add).then_inc(y_done, 1)

                def step(c, first, last):
                    update_state(c)
                    dve.wait_ge(sg_loaded, 16 * c + 16)
                    gate_o(c, sg, og)
                    if not last:
                        prepare(c + 1)
                    if not first:
                        dve.wait_ge(x_loaded, 16 * c)
                        finish(c - 1, x, gate, y)
                    if not last:
                        mask(c + 1)
                    low(c)

                dve.sem_inc(y_done, 1)
                dve.sem_inc(x1_stored, 16)
                dve.memset(S[:, :, :], 0.0).then_inc(s_ready, 1)
                for tile in (q_far, k_far, q_one):
                    dve.memset(tile[:, :, :], 0.0).then_inc(cleared, 1)
                prepare(0)
                mask(0)
                dve.wait_ge(small_loaded, 16 * (DV // P))
                split_output_weight(None, dve, w_raw, w_hi, w_lo, w_loaded, w_hi_done, w_ready, K,
                                    [onorm[:, kk % (DV // P):kk % (DV // P) + 1] for kk in range(K)], w_scaled)
                dve.wait_ge(gate_loaded, 16)
                steps(dve, step)
                dve.wait_ge(x_loaded, 16 * NT)
                finish(NT - 1, x, gate, y)
                for part in (oT_hi, oT_lo):
                    dve.memset(part[:, :, :].bitcast(F32), 0.0).then_inc(cleared, 1)
                dve.wait_ge(small_loaded, 16 * (DV // P + 6))
                for hh in range(HA):
                    op = dve.tensor_copy(q_one[:, hh, 0:NS * NS:NS + 1], qs[:, hh * NS:(hh + 1) * NS])
                op.then_inc(q_one_ready, 2)
                dve.wait_ge(a_ready, 1)
                for s in range(NS):
                    u = s % 2
                    dve.wait_ge(s_loaded[u], 16 * (s // 2 + 1))
                    dve.wait_ge(v_all_loaded[u], 16 * (s // 2 + 1))
                    if s >= 2:
                        dve.wait_ge(s_used, s - 1)
                        dve.wait_ge(s_stored[u], 16 * (s // 2))
                    for hh in range(HA):
                        cols, at = slice(hh * DV, (hh + 1) * DV), hh * NS + s
                        dve.tensor_scalar(v_all[u][:, cols], v_all[u][:, cols], ks[:, at:at + 1], None, ALU.mult)\
                           .then_inc(s_chain, 1)
                    dve.wait_ge(s_chain, HA * (s + 1))
                    for hh in range(HA):
                        cols, at = slice(hh * DV, (hh + 1) * DV), hh * NS + s
                        op = dve.scalar_tensor_tensor(s_out[u][:, hh, :], s_in[u][:, hh, :], as_[:, at:at + 1],
                                                      v_all[u][:, cols], ALU.mult, ALU.add)
                    op.then_inc(s_made, 1)
                gate_o(NT, sg_s, og_s, NS)
                dve.wait_ge(oT_hi_done, 2 * NT + 2)
                dve.wait_ge(cleared, 5)
                dve.tensor_tensor(oT_lo[:, :, 0:NS], g.bank[4][:, 0:K * NS].rearrange("p (k c) -> p k c", c=NS),
                                  oT_hi[:, :, 0:NS].bitcast(F32), ALU.subtract).then_inc(oT_lo_done, 2)
                finish(NT, x_s, gate_s, y_s, NS)


def kv_projections(nc, g):
    with ExitStack() as st:
        norm = st.enter_context(nc.sbuf_tensor("k_norm_rows", [P, g.HD], F32))[:, :]
        bias = st.enter_context(nc.sbuf_tensor("b_f_rows", [P, g.HB], F32))[:, :]
        row = lambda a: a.rearrange("(a n) -> a n", a=1)
        loads = [(norm, row(g.i.k_norm).broadcast_to([P, g.HD])), (bias, row(g.i.b_f).broadcast_to([P, g.HB]))]
        flat = lambda a: a.rearrange("t h d -> t (h d)")
        w, o, blocks = g.i.w_kv, g.o, g.D // NB
        plan = [group("headnorm", w, 0, blocks, flat(o.k_prompt[0]), flat(o.k_sample[:, 0]), norm=norm),
                group("plain", w, blocks, blocks, flat(o.v_prompt[0]), flat(o.v_sample[:, 0])),
                group("logf", w, 2 * blocks, 1, o.logf_prompt[0], o.logf_sample[:, 0], width=g.HB, bias=bias)]
        projection_phase(nc, g, "kv", g.x1, g.x1_s, g.mod_kv, g.mod_kv + g.K, plan, loads)


def fox_projections(nc, g):
    with ExitStack() as st:
        norm = st.enter_context(nc.sbuf_tensor("q_norm_rows", [P, g.HD], F32))[:, :]
        w, blocks = g.i.fox_w_in[0], g.D // NB
        plan = [group("headnorm", w, 0, blocks, g.q_fox, g.q_fox_s, norm=norm, scale=float(g.HD) ** -0.5),
                group("silu", w, blocks, blocks, g.sg_fox, g.sg_fox_s)]
        projection_phase(nc, g, "fox", g.x1, g.x1_s, g.mod_fox, g.mod_fox + g.K, plan,
                         [(norm, g.i.q_norm[0:1, :].broadcast_to([P, g.HD]))])


def forget_sums(nc, g):
    T, NT, HB, NG = g.T, g.NT, g.HB, g.T // NB
    with ExitStack() as st:
        sb = lambda n, s, d=F32: st.enter_context(nc.sbuf_tensor(f"fs_{n}", s, d))
        lf, in_tile, F = sb("lf", [HB, T]), sb("in_tile", [HB, T]), sb("F", [HB, T])
        totals, ones = sb("totals", [HB, NT]), sb("ones", [HB, NT])
        f_hi, f_lo = sb("f_hi", [HB, T], F32R), sb("f_lo", [HB, T], F32R)
        turned, lf_ready, masks, chain = g.sem("fs_turned"), g.sem("fs_lf_ready"), g.sem("fs_masks"), g.sem("fs_chain")
        stored = g.sem("fs_stored")
        tiles = lambda a: a[:, :].rearrange("p (t c) -> p t c", c=P)
        with nc.Block() as block:
            @block.tensor
            def _(pe):
                for t in range(NT):
                    mm = pe.matmul(g.bank[t // 4][0:HB, t % 4 * P:(t % 4 + 1) * P],
                                   g.logf_all[:, t * HB:(t + 1) * HB], g.ident[:, :], start=True, stop=True)
                    if t % 4 == 3:
                        mm.then_inc(turned, 1)

            @block.gpsimd
            def _(pool):
                pool.memset(in_tile[:, :], 1.0).then_inc(masks, 1)
                pool.memset(ones[:, :], 1.0).then_inc(masks, 1)
                pool.wait_ge(masks, 2)
                pool.memset(tiles(in_tile)[:, :, 0:1], 0.0).then_inc(masks, 1)

            @block.vector
            def _(dve):
                for b in range(NG):
                    dve.wait_ge(turned, b + 1)
                    dve.tensor_copy(lf[:, b * NB:(b + 1) * NB], g.bank[b][0:HB, :]).then_inc(lf_ready, 1)
                dve.wait_ge(lf_ready, NG)
                dve.wait_ge(masks, 3)
                dve.tensor_tensor_scan(F[:, :], in_tile[:, :], lf[:, :], 0.0, ALU.mult, ALU.add).then_inc(chain, 1)
                dve.wait_ge(chain, 1)
                dve.tensor_tensor_scan(totals[:, :], ones[:, :], tiles(F)[:, :, P - 1], 0.0, ALU.mult, ALU.add)\
                   .then_inc(chain, 1)
                dve.wait_ge(chain, 2)
                dve.tensor_tensor(tiles(F)[:, 1:, :], tiles(F)[:, 1:, :],
                                  totals[:, 0:NT - 1].unsqueeze(2).broadcast_to([HB, NT - 1, P]), ALU.add)\
                   .then_inc(chain, 1)
                dve.wait_ge(chain, 3)
                dve.tensor_scalar(f_hi[:, :], F[:, :], -1.0, None, ALU.mult).then_inc(chain, 1)
                dve.wait_ge(chain, 4)
                dve.scalar_tensor_tensor(f_lo[:, :], F[:, :], -1.0, f_hi[:, :].bitcast(F32), ALU.mult, ALU.subtract)\
                   .then_inc(chain, 1)

            @block.sync
            def _(sp):
                sp.wait_ge(chain, 5)
                sp.dma_start(g.f_hi, f_hi[:, :].bitcast(F32)).then_inc(stored, 16)
                sp.dma_start(g.f_lo, f_lo[:, :].bitcast(F32)).then_inc(stored, 16)
                sp.wait_ge(stored, 32)


def attention_phase(nc, g):
    T, NT, HD, HB, NG = g.T, g.NT, g.HD, g.HB, g.T // NB
    R = NB // P
    VC = HD + 2
    exp_units = [(G, i) for G in range(NG) for i in range(R * G + R)]
    UN = len(exp_units)
    ends = lambda e: e > 0 and exp_units[e][1] == 0
    units_to = lambda G: R * (G + 1) * (G + 2) // 2
    TU = 3 * NG
    fillers = [("turn", 0, 0), ("turn", 0, 1)]
    for G in range(NG):
        maxima = [("max", t, c) for t in range(R * G, R * G + R) for c in range(G + 1)]
        if G:
            maxima.insert(2, ("m_row", G - 1, 0))
        if G + 1 < NG:
            maxima.insert(1, ("turn", G + 1, 0))
            maxima.insert(5 if G else 3, ("turn", G + 1, 1))
        fillers += maxima + [("m_max", G, 0)]
    fillers.append(("m_row", NG - 1, 0))
    counts, turn = {"max": 0, "turn": 0}, []
    for kind, a, b in fillers:
        uses = {"turn": "turn", "m_row": "turn", "max": "max"}.get(kind)
        turn.append((kind, a, b, counts.get(uses)))
        if uses:
            counts[uses] += 1
    fillers = turn
    cut = [0, 2, 2] + [2 + (e * (len(fillers) - 5) + UN - 4) // (UN - 3) for e in range(UN - 2)]
    dve_fillers = list(fillers)
    for n in range(len(fillers) - 2, 1, -1):
        if dve_fillers[n][0] == "turn" and dve_fillers[n + 1][0] == "max":
            dve_fillers[n], dve_fillers[n + 1] = dve_fillers[n + 1], dve_fillers[n]
    PAIRS = HB // 2
    PG = g.PAGES
    assert PG == 4 and PAIRS == g.NS
    page_at = [1 + n * (UN - 2) // 8 for n in range(8)]
    with ExitStack() as st:
        sb = lambda n, s, d=F32: st.enter_context(nc.sbuf_tensor(f"at_{n}", s, d))
        sem = lambda n: g.sem(f"at_{n}")
        rows = [sb(f"{n}_rows", [P, NT, P]) for n in "qk"]
        hi = [[sb(f"{n}T_hi{u}", [P, T], F32R) for u in range(2)] for n in "qk"]
        lo = [[sb(f"{n}T_lo{u}", [P, T], F32R) for u in range(2)] for n in "qk"]
        v = [sb(f"v{u}", [P, NT, VC]) for u in range(2)]
        p_tile = [sb(f"p{s}", [P, NB]) for s in range(4)]
        chunk_max = sb("chunk_max", [P, R, NG])
        m = sb("m", [P, R])
        m_hi, m_lo = sb("m_hi", [R, P], F32R), sb("m_lo", [R, P], F32R)
        o_sum = [sb(f"o_sum{s}", [P, R]) for s in range(2)]
        oT = [sb(f"oT{s}", [HD + 1, NB]) for s in range(2)]
        o = [sb(f"o{s}", [P, R, HD]) for s in range(2)]
        q_samples = sb("q_samples", [P, g.NS, g.D])
        page = [sb(f"page{w}", [P, g.D]) for w in range(2)]
        table = sb("table", [1, g.NS * PG], I32)
        data = [slice(0, HD), slice(HD, P)]
        depth = [slice(0, HD + 2), slice(0, P)]
        M_ROW, EXTRA = [HD, 0], [slice(HD, HD + 2), slice(0, 2)]
        F_ROW = [HD + 1, 1]

        cleared, m_cleared = sem("cleared"), sem("m_cleared")
        rows_loaded, f_loaded = sem("rows_loaded"), sem("f_loaded")
        v_loaded = [sem(f"v_loaded{u}") for u in range(2)]
        turn_full, turn_hi, turn_used = sem("turn_full"), sem("turn_hi"), sem("turn_used")
        max_full, max_done, m_ready, m_chain = sem("max_full"), sem("max_done"), sem("m_ready"), sem("m_chain")
        m_stored = sem("m_stored")
        st_full, p_ready, p_used = sem("st_full"), sem("p_ready"), sem("p_used")
        oT_ready, o_turned, o_chain, o_done = sem("oT_ready"), sem("o_turned"), sem("o_chain"), sem("o_done")
        o_stored = [sem(f"o_stored{s}") for s in range(2)]
        table_loaded, q_samples_loaded, lf_loaded = sem("table_loaded"), sem("q_samples_loaded"), sem("lf_loaded")
        page_loaded = [sem(f"page_loaded{w}") for w in range(2)]
        page_prod, page_done = sem("page_prod"), sem("page_done")
        bank_turn, bank_max, bank_st, bank_o = g.bank[0:2], g.bank[2:4], g.bank[4:6], g.bank[6:8]

        def steps(eng, step):
            if PAIRS > 1:
                with eng.Fori(0, PAIRS - 1) as j:
                    step(j, 0, True)
                    step(j, 1, True)
            step(PAIRS - 1, 0, True)
            step(PAIRS - 1, 1, False)

        def following(j, u):
            return (j, 1) if u == 0 else (j + 1, 0)

        clears = [(part[b][1][:, :].bitcast(F32), 0.0) for part in (hi, lo) for b in range(2)]
        clears += [(lo[b][0][EXTRA[0], :].bitcast(F32), 0.0) for b in range(2)]
        clears += [(hi[b][u][EXTRA[u], :].bitcast(F32), 1.0) for u in range(2) for b in range(2)]
        clears += [(v[u][:, :, HD:VC], 1.0) for u in range(2)]

        with nc.Block() as block:
            @block.sync
            def _(sp):
                def load_rows(j):
                    for tile, src in zip(rows, (g.q_fox, g.k_rows)):
                        sp.dma_start(tile[:, :, :], src.rearrange("(t p) n -> p t n", p=P)[:, :, ds(j * P, P)])\
                            .then_inc(rows_loaded, 16)

                def load_v(j, u):
                    sp.dma_start(v[u][:, :, 0:HD], g.v_rows.rearrange("(t p) n -> p t n", p=P)
                                 [:, :, ds((2 * j + u) * HD, HD)]).then_inc(v_loaded[u], 16)

                def load_f(j, u):
                    sp.wait_ge(turn_full, TU * (2 * j + u) + 1)
                    for part, src in ((hi, g.f_hi), (lo, g.f_lo)):
                        sp.dma_start(part[1][u][F_ROW[u]:F_ROW[u] + 1, :].bitcast(F32), src[ds(2 * j + u, 1), :])\
                            .then_inc(f_loaded, 16)

                def filler(j, u, kind, G, b, n):
                    if (kind, G, b, u) == ("turn", NG - 1, 1, 1) and not last_pair(j):
                        sp.wait_ge(turn_full, TU * (2 * j + u) + n + 1)
                        load_rows(j + 1)
                    if kind != "m_row":
                        return
                    sp.wait_ge(turn_used, TU * (2 * j + u) + n + 1 + 2)
                    for part, src in ((hi, m_hi), (lo, m_lo)):
                        sp.dma_start(part[0][u][M_ROW[u]:M_ROW[u] + 1, G * NB:(G + 1) * NB].bitcast(F32)
                                     .rearrange("a (r c) -> a r c", c=P), src[:, :].bitcast(F32)).then_inc(m_stored, 16)

                def store_o(j, u, G):
                    sp.wait_ge(o_done, NG * (2 * j + u) + G + 1 + 2)
                    s = (NG * u + G) % 2
                    sp.dma_start(g.o_fox.rearrange("(g r p) n -> g p r n", r=R, p=P)[G][:, :, ds((2 * j + u) * HD, HD)],
                                 o[s][:, :, :]).then_inc(o_stored[s], 16)

                def step(j, u, more):
                    if more:
                        load_f(*following(j, u))
                        load_v(*following(j, u))
                    for e in range(UN):
                        if more:
                            for f in fillers[cut[e]:cut[e + 1]]:
                                filler(*following(j, u), *f)
                        if ends(e - 1):
                            store_o(j, u, exp_units[e][0] - 1)
                        if more and e in (page_at[3], page_at[7]):
                            load_page(*following(j, u), page_at.index(e) // 4)
                    store_o(j, u, NG - 1)
                    if more:
                        filler(*following(j, u), *fillers[-1])

                def load_page(j, u, w):
                    number = sp.value_load(table[0:1, ds(PG * j + 2 * u + w, 1)], min_val=0, max_val=g.POOL - 1)
                    sp.dma_start(g.lf_pages[:, 2 * u + w, ds(j * HB, HB)],
                                 g.i.cache_logf[ds(number, 1)].rearrange("a s h -> (a s) h")).then_inc(lf_loaded, 16)
                    sp.wait_ge(page_done, 4 * (2 * j + u) + 2 * w + 2)
                    sp.dma_start(page[w][:, :], g.i.cache_k[ds(number, 1)].rearrange("a s h d -> (a s) (h d)"))\
                        .then_inc(page_loaded[w], 16)

                last_pair = lambda j: isinstance(j, int) and j == PAIRS - 1
                sp.dma_start(table[:, :], g.i.page_table.rearrange("(a b) n -> a (b n)", a=1)).then_inc(table_loaded, 16)
                load_rows(0)
                load_v(0, 0)
                sp.wait_ge(cleared, len(clears))
                load_f(0, 0)
                for f in fillers:
                    filler(0, 0, *f)
                sp.dma_start(q_samples[:, :, :].rearrange("p b n -> p (b n)"),
                             g.q_fox_s.rearrange("(a b) n -> a (b n)", a=1).broadcast_to([P, g.NS * g.D]))\
                    .then_inc(q_samples_loaded, 16)
                sp.wait_ge(table_loaded, 16)
                for w in range(2):
                    load_page(0, 0, w)
                steps(sp, step)
                sp.wait_ge(lf_loaded, 16 * g.NS * PG)
                for s in range(2):
                    sp.wait_ge(o_stored[s], 16 * (HB * NG // 2 + 1))

            @block.tensor
            def _(pe):
                def filler(j, u, kind, a, b, n):
                    h = 2 * j + u
                    if kind == "turn":
                        pe.wait_ge(turn_used, TU * h + n + 1)
                        bank = bank_turn[(TU * u + n) % 2]
                        for r in range(R):
                            mm = pe.matmul(bank[:, r * P:(r + 1) * P], rows[b][:, R * a + r, :], g.ident[:, :],
                                           is_transpose=True, start=True, stop=True)
                        mm.then_inc(turn_full, 1)
                    if kind == "max":
                        t, c = a, b
                        w = min(NB, (t + 1) * P - c * NB)
                        if t % R == 0 and c == 0:
                            pe.wait_ge(turn_hi, 2 * NG * h + 2 * (t // R) + 2)
                        pe.wait_ge(max_done, UN * h + n + 1)
                        bank = bank_max[n % 2]
                        diagonal = c == t // R
                        mm = pe.matmul(bank[:, 0:w], hi[0][u][depth[u], t * P:(t + 1) * P],
                                       hi[1][u][depth[u], c * NB:c * NB + w], start=True, stop=not diagonal)
                        if diagonal:
                            mm = pe.matmul(bank[:, w - P:w], g.ident16[:, :], g.hide_qk[:, :], start=False, stop=True)
                        mm.then_inc(max_full, 1)
                    if kind == "m_row":
                        pe.wait_ge(m_ready, NG * h + a + 1 + 1)
                        pe.wait_ge(turn_used, TU * h + n + 1)
                        pe.matmul(bank_turn[(TU * u + n) % 2][0:R, 0:P], m[:, :], g.ident[:, :], start=True, stop=True)\
                          .then_inc(turn_full, 1)

                def logits(j, u, e):
                    h = 2 * j + u
                    G, i = exp_units[e]
                    skip = max(0, i - R * G) * P
                    if i == 0:
                        pe.wait_ge(m_stored, 32 * (NG * h + G) + 32 + 32)
                    pe.wait_ge(p_ready, UN * h + e + 1)
                    bank = bank_st[e % 2]
                    keys, queries = slice(i * P, (i + 1) * P), slice(G * NB + skip, (G + 1) * NB)
                    k_part = [part[1][u][depth[u], keys] for part in (hi, lo)]
                    q_part = [part[0][u][depth[u], queries] for part in (hi, lo)]
                    diagonal = i >= R * G
                    pe.matmul(bank[:, skip:NB], k_part[0], q_part[0], start=True, stop=False)
                    pe.matmul(bank[:, skip:NB], k_part[0], q_part[1], start=False, stop=False)
                    mm = pe.matmul(bank[:, skip:NB], k_part[1], q_part[0], start=False, stop=not diagonal)
                    if diagonal:
                        mm = pe.matmul(bank[:, skip:skip + P], g.ident16[:, :], g.hide_kq[:, :], start=False, stop=True)
                    mm.then_inc(st_full, 1)

                def weigh_v(j, u, e):
                    h = 2 * j + u
                    G, i = exp_units[e]
                    if e == 0:
                        pe.wait_ge(v_loaded[u], 16 * j + 16)
                    if i == 0:
                        pe.wait_ge(o_done, NG * h + G + 1)
                    pe.wait_ge(p_ready, UN * h + e + 1 + 2)
                    skip = max(0, i - R * G) * P
                    pe.matmul(bank_o[(NG * u + G) % 2][0:HD + 1, skip:NB], v[u][:, i, 0:HD + 1], p_tile[e % 4][:, skip:NB],
                              start=(i == 0), stop=(i == R * G + R - 1), skip_group_check=True).then_inc(p_used, 1)

                def turn_o(j, u, G):
                    s = (NG * u + G) % 2
                    pe.wait_ge(oT_ready, NG * (2 * j + u) + G + 1)
                    for r in range(R):
                        mm = pe.transpose(bank_o[s][:, r * VC:r * VC + HD + 1], oT[s][:, r * P:(r + 1) * P],
                                          g.ident[0:HD + 1, 0:HD + 1])
                    mm.then_inc(o_turned, 1)

                def step(j, u, more):
                    for e in range(UN):
                        logits(j, u, e)
                        if e:
                            weigh_v(j, u, e - 1)
                        if more:
                            for f in fillers[cut[e]:cut[e + 1]]:
                                prepare(*following(j, u), *f)
                        if ends(e - 1):
                            turn_o(j, u, exp_units[e][0] - 1)
                    weigh_v(j, u, UN - 1)
                    if more:
                        for f in fillers[cut[UN]:-1]:
                            prepare(*following(j, u), *f)
                    turn_o(j, u, NG - 1)
                    if more:
                        prepare(*following(j, u), *fillers[-1])

                def prepare(j, u, kind, a, b, n):
                    if n == 0 and kind == "turn":
                        pe.wait_ge(rows_loaded, 32 * j + 32)
                    if n == 0 and kind == "max":
                        pe.wait_ge(f_loaded, 32 * (2 * j + u) + 32)
                    if kind == "max" and a % R == 0 and b == 0:
                        pe.wait_ge(m_cleared, NG * (2 * j + u) + a // R + 1)
                    filler(j, u, kind, a, b, n)

                pe.sem_inc(p_used, 4)
                pe.wait_ge(cleared, len(clears))
                for f in fillers:
                    prepare(0, 0, *f)
                steps(pe, step)

            @block.scalar
            def _(act):
                def filler(j, u, kind, a, b, n):
                    if kind != "turn":
                        return
                    act.wait_ge(turn_full, TU * (2 * j + u) + n + 1)
                    act.activation(hi[b][u][data[u], a * NB:(a + 1) * NB], bank_turn[(TU * u + n) % 2][data[u], :],
                                   ACT.Copy).then_inc(turn_hi, 1)

                def exponential(j, u, e):
                    G, i = exp_units[e]
                    skip = max(0, i - R * G) * P
                    act.wait_ge(st_full, UN * (2 * j + u) + e + 1)
                    act.wait_ge(p_used, UN * (2 * j + u) + e + 1)
                    act.activation(p_tile[e % 4][:, skip:NB], bank_st[e % 2][:, skip:NB], ACT.Exp).then_inc(p_ready, 1)

                def copy_o(j, u, G):
                    s = (NG * u + G) % 2
                    act.wait_ge(p_used, UN * (2 * j + u) + units_to(G) + 4)
                    act.activation(oT[s][:, :], bank_o[s][0:HD + 1, :], ACT.Copy).then_inc(oT_ready, 1)

                def step(j, u, more):
                    for e in range(UN):
                        exponential(j, u, e)
                        if ends(e):
                            copy_o(j, u, exp_units[e][0] - 1)
                        if more:
                            for f in fillers[cut[e]:cut[e + 1]]:
                                filler(*following(j, u), *f)
                    copy_o(j, u, NG - 1)
                    if more:
                        for f in fillers[cut[UN]:]:
                            filler(*following(j, u), *f)

                act.sem_inc(p_ready, 2)
                act.wait_ge(cleared, len(clears))
                for f in fillers:
                    filler(0, 0, *f)
                steps(act, step)

            @block.vector
            def _(dve):
                def filler(j, u, kind, a, b, n):
                    h = 2 * j + u
                    if kind == "turn":
                        dve.wait_ge(turn_hi, 2 * NG * h + 2 * a + b + 1)
                        cols = slice(a * NB, (a + 1) * NB)
                        dve.tensor_tensor(lo[b][u][data[u], cols], bank_turn[(TU * u + n) % 2][data[u], :],
                                          hi[b][u][data[u], cols].bitcast(F32), ALU.subtract).then_inc(turn_used, 1)
                    if kind == "max":
                        t, c = a, b
                        w = min(NB, (t + 1) * P - c * NB)
                        if t % R == 0 and c == 0:
                            dve.wait_ge(m_ready, NG * h + t // R + 1)
                        dve.wait_ge(max_full, UN * h + n + 1)
                        dve.tensor_reduce(chunk_max[:, t % R, c:c + 1], bank_max[n % 2][:, 0:w], AX.X, ALU.max)\
                           .then_inc(max_done, 1)
                    if kind == "m_max":
                        G = a
                        dve.wait_ge(max_done, UN * h + units_to(G) + 2)
                        dve.tensor_reduce(m[:, :], chunk_max[:, :, 0:G + 1], AX.X, ALU.max).then_inc(m_ready, 1)
                    if kind == "m_row":
                        G = a
                        dve.wait_ge(turn_full, TU * h + n + 1)
                        dve.wait_ge(m_stored, 32 * (NG * h + G) + 32)
                        src = bank_turn[(TU * u + n) % 2][0:R, 0:P]
                        dve.tensor_scalar(m_hi[:, :], src, -1.0, None, ALU.mult).then_inc(m_chain, 1)
                        dve.wait_ge(m_chain, NG * h + G + 1)
                        dve.scalar_tensor_tensor(m_lo[:, :], src, -1.0, m_hi[:, :].bitcast(F32), ALU.mult, ALU.subtract)\
                           .then_inc(turn_used, 1)

                def score_page(j, u, n):
                    h, w, half = 2 * j + u, n // 4, n % 2
                    cols = slice(half * NB, (half + 1) * NB)
                    if n % 4 == 0:
                        dve.wait_ge(page_loaded[w], 16 * h + 16)
                    if n % 4 < 2:
                        dve.tensor_tensor(page[w][:, cols], page[w][:, cols],
                                          q_samples[:, ds(j, 1), cols].rearrange("p a n -> p (a n)"), ALU.mult)\
                           .then_inc(page_prod, 1)
                    else:
                        dve.wait_ge(page_prod, 4 * h + 2 * w + 2)
                        heads = NB // HD
                        dve.tensor_reduce(g.scores[:, 2 * u + w, ds(j * HB + half * heads, heads)],
                                          page[w][:, cols].rearrange("p (h d) -> p h d", d=HD), AX.X, ALU.add)\
                           .then_inc(page_done, 1)

                def finish(j, u, G):
                    h = 2 * j + u
                    s = (NG * u + G) % 2
                    ps = bank_o[s][:, 0:R * VC].rearrange("p (r c) -> p r c", c=VC)
                    dve.wait_ge(o_turned, NG * h + G + 1)
                    dve.wait_ge(o_stored[s], 16 * (NG * j) + 16 * ((NG * u + G) // 2) + 16)
                    dve.reciprocal(o_sum[s][:, :].unsqueeze(2), ps[:, :, HD:HD + 1]).then_inc(o_chain, 1)
                    dve.wait_ge(o_chain, NG * h + G + 1)
                    dve.tensor_tensor(o[s][:, :, :], ps[:, :, 0:HD],
                                      o_sum[s][:, :].unsqueeze(2).broadcast_to([P, R, HD]), ALU.mult).then_inc(o_done, 1)

                def step(j, u, more):
                    for e in range(UN):
                        if more:
                            for f in dve_fillers[cut[e]:cut[e + 1]]:
                                filler(*following(j, u), *f)
                        if ends(e - 1):
                            finish(j, u, exp_units[e][0] - 1)
                        if e in page_at:
                            score_page(j, u, page_at.index(e))
                    if more:
                        for f in dve_fillers[cut[UN]:-1]:
                            filler(*following(j, u), *f)
                    finish(j, u, NG - 1)
                    if more:
                        filler(*following(j, u), *dve_fillers[-1])

                dve.sem_inc(turn_used, 2)
                dve.sem_inc(max_done, 2)
                dve.sem_inc(m_ready, 1)
                dve.sem_inc(m_stored, 32)
                dve.sem_inc(page_done, 4)
                dve.sem_inc(o_done, 2)
                for s in range(2):
                    dve.sem_inc(o_stored[s], 16)
                dve.wait_ge(cleared, len(clears))
                for f in dve_fillers:
                    filler(0, 0, *f)
                dve.wait_ge(q_samples_loaded, 16)
                steps(dve, step)

            @block.gpsimd
            def _(pool):
                for n, (tile, value) in enumerate(clears):
                    if n:
                        pool.wait_ge(cleared, n)
                    pool.memset(tile, value).then_inc(cleared, 1)

                def clear_m(u):
                    for G in range(NG):
                        cols = slice(G * NB, (G + 1) * NB)
                        zero = lo[1][u][M_ROW[u]:M_ROW[u] + 1, cols].bitcast(F32)
                        pool.tensor_tensor(hi[0][u][M_ROW[u]:M_ROW[u] + 1, cols], zero, zero, ALU.add).then_inc(m_cleared, 1)

                def step(j, u, more):
                    if more:
                        pool.wait_ge(p_used, UN * (2 * j + u) + 4)
                        clear_m(1 - u)
                pool.wait_ge(cleared, len(clears))
                clear_m(0)
                steps(pool, step)


def sample_attention(nc, g):
    NS, HB, HD, D, PG = g.NS, g.HB, g.HD, g.D, g.PAGES
    S = PG * P
    with ExitStack() as st:
        sb = lambda n, s, d=F32: st.enter_context(nc.sbuf_tensor(f"sa_{n}", s, d))
        sem = lambda n: g.sem(f"sa_{n}")
        v_page = [sb(f"v_page{s}", [P, D]) for s in range(PG)]
        table = sb("table", [1, NS * PG], I32)
        scores, lf = g.scores, g.lf_pages
        q_row, k_row, lf_row = sb("q_row", [P, HD]), sb("k_row", [P, HD]), sb("lf_row", [P, 1])
        logit = sb("logit", [P, S + 1])
        F, totals = sb("F", [P, PG, P]), sb("totals", [P, PG])
        in_page, ones = sb("in_page", [P, PG, P]), sb("ones", [P, PG])
        m, total, share = sb("m", [P, 1]), sb("total", [P, 1]), sb("share", [P, 1])
        pT = sb("pT", [P, PG, P])
        oT = sb("oT", [P, D // P, NS])
        p_new, v_new, o = sb("p_new", [NS, HB]), sb("v_new", [NS, D]), sb("o", [NS, D])
        loaded, table_loaded = sem("loaded"), sem("table_loaded")
        v_loaded = [sem(f"v_loaded{s}") for s in range(PG)]
        v_used = sem("v_used")
        masks, turned, chain, prob, p_turned = sem("masks"), sem("turned"), sem("chain"), sem("prob"), sem("p_turned")
        pT_ready, new_moved, o_taken, o_turned = sem("pT_ready"), sem("new_moved"), sem("o_taken"), sem("o_turned")
        o_chain, stored = sem("o_chain"), sem("stored")
        heads = lambda a: a.rearrange("p (h d) -> p h d", d=HD)

        with nc.Block() as block:
            @block.sync
            def _(sp):
                sp.dma_start(table[:, :], g.i.page_table.rearrange("(a b) n -> a (b n)", a=1)).then_inc(table_loaded, 16)
                sp.wait_ge(table_loaded, 16)

                for tile, src in ((q_row, g.q_fox_s.rearrange("b (h d) -> (b h) d", d=HD)),
                                  (k_row, g.o.k_sample.rearrange("b a h d -> (b a h) d")),
                                  (lf_row, g.o.logf_sample.rearrange("b a (h c) -> (b a h) c", c=1)),
                                  (v_new, g.o.v_sample.rearrange("b a h d -> (b a) (h d)"))):
                    sp.dma_start(tile[:, :], src).then_inc(loaded, 16)
                with sp.Fori(0, NS) as b:
                    for s in range(PG // 2):
                        number = sp.value_load(table[0:1, ds(PG * b + s, 1)], min_val=0, max_val=g.POOL - 1)
                        sp.wait_ge(v_used, PG * b + s + 1)
                        sp.dma_start(v_page[s][:, :], g.i.cache_v[ds(number, 1)].rearrange("a s h d -> (a s) (h d)"))\
                            .then_inc(v_loaded[s], 16)
                sp.wait_ge(chain, 12)
                sp.dma_start(p_new[:, :], logit[:, S:S + 1]).then_inc(new_moved, 16)
                sp.wait_ge(o_chain, 3)
                sp.dma_start(g.o_fox_s, o[:, :]).then_inc(stored, 16)
                sp.wait_ge(stored, 16)

            @block.gpsimd
            def _(pool):
                pool.memset(in_page[:, :, :], 1.0).then_inc(masks, 1)
                pool.memset(ones[:, :], 1.0).then_inc(masks, 1)
                pool.wait_ge(masks, 2)
                pool.memset(in_page[:, :, 0:1], 0.0).then_inc(masks, 1)
                pool.wait_ge(table_loaded, 16)
                with pool.Fori(0, NS) as b:
                    for s in range(PG // 2, PG):
                        number = pool.value_load(table[0:1, ds(PG * b + s, 1)], min_val=0, max_val=g.POOL - 1)
                        pool.wait_ge(v_used, PG * b + s + 1)
                        pool.dma_start(v_page[s][:, :], g.i.cache_v[ds(number, 1)].rearrange("a s h d -> (a s) (h d)"))\
                            .then_inc(v_loaded[s], 16)

            @block.tensor
            def _(pe):
                for s in range(PG):
                    pe.transpose(g.bank[0][:, s * P:(s + 1) * P], lf[:, s, :], g.ident[:, :])
                    mm = pe.transpose(g.bank[1][:, s * P:(s + 1) * P], scores[:, s, :], g.ident[:, :])
                mm.then_inc(turned, 1)
                pe.wait_ge(chain, 12)
                for s in range(PG):
                    mm = pe.transpose(g.bank[2][:, s * P:(s + 1) * P], logit[:, s * P:(s + 1) * P], g.ident[:, :])
                mm.then_inc(p_turned, 1)
                pe.sem_inc(v_used, PG)
                pe.wait_ge(pT_ready, 1)
                with pe.Fori(0, NS // 2) as h:
                    for u in range(2):
                        b = 2 * h + u
                        pe.wait_ge(o_taken, 2 * b + 2)
                        for s in range(PG):
                            pe.wait_ge(v_loaded[s], 16 * b + 16)
                            for c in range(D // P):
                                mm = pe.matmul(g.bank[4 + u][:, c * HB:(c + 1) * HB], v_page[s][:, c * P:(c + 1) * P],
                                               pT[:, s, ds(b * HB, HB)], start=(s == 0 and c == 0), stop=(s == PG - 1),
                                               skip_group_check=True)
                            mm.then_inc(v_used, 1)
                pe.wait_ge(o_taken, 2 * NS + 4)
                for c in range(D // P):
                    mm = pe.matmul(g.bank[6 + c // 4][0:NS, c % 4 * P:(c % 4 + 1) * P], oT[:, c, :], g.ident[:, :],
                                   start=True, stop=True)
                mm.then_inc(o_turned, 1)

            @block.scalar
            def _(act):
                act.wait_ge(chain, 10)
                act.activation(logit[:, :], logit[:, :], ACT.Exp, accum_out=total[:, :]).then_inc(prob, 1)

            @block.vector
            def _(dve):
                dve.sem_inc(o_taken, 4)
                pages = lambda a: a[:, 0:S].rearrange("p (n c) -> p n c", c=P)
                dve.wait_ge(loaded, 64)
                dve.wait_ge(masks, 3)
                dve.wait_ge(turned, 1)
                dve.tensor_tensor(q_row[:, :], q_row[:, :], k_row[:, :], ALU.mult).then_inc(chain, 1)
                dve.wait_ge(chain, 1)
                dve.tensor_reduce(logit[:, S:S + 1], q_row[:, :], AX.X, ALU.add).then_inc(chain, 1)
                dve.wait_ge(chain, 2)
                flat = lambda a: a[:, :, :].rearrange("p n c -> p (n c)")
                dve.tensor_tensor_scan(flat(F), flat(in_page), g.bank[0][:, 0:S], 0.0, ALU.mult, ALU.add).then_inc(chain, 1)
                dve.wait_ge(chain, 3)
                dve.tensor_tensor_scan(totals[:, :], ones[:, :], F[:, :, P - 1], 0.0, ALU.mult, ALU.add).then_inc(chain, 1)
                dve.wait_ge(chain, 4)
                dve.tensor_tensor(pages(logit), g.bank[1][:, 0:S].rearrange("p (n c) -> p n c", c=P), F[:, :, :],
                                  ALU.subtract).then_inc(chain, 1)
                dve.wait_ge(chain, 5)
                dve.tensor_tensor(pages(logit)[:, 1:, :], pages(logit)[:, 1:, :],
                                  totals[:, 0:PG - 1].unsqueeze(2).broadcast_to([P, PG - 1, P]), ALU.subtract).then_inc(chain, 1)
                dve.wait_ge(chain, 6)
                dve.tensor_tensor(lf_row[:, :], lf_row[:, :], totals[:, PG - 1:PG], ALU.add).then_inc(chain, 1)
                dve.wait_ge(chain, 7)
                dve.tensor_tensor(logit[:, S:S + 1], logit[:, S:S + 1], lf_row[:, :], ALU.subtract).then_inc(chain, 1)
                dve.wait_ge(chain, 8)
                dve.tensor_reduce(m[:, :], logit[:, :], AX.X, ALU.max).then_inc(chain, 1)
                dve.wait_ge(chain, 9)
                dve.tensor_scalar(logit[:, :], logit[:, :], m[:, :], None, ALU.subtract).then_inc(chain, 1)
                dve.wait_ge(chain, 10)
                dve.wait_ge(prob, 1)
                dve.reciprocal(share[:, :], total[:, :]).then_inc(chain, 1)
                dve.wait_ge(chain, 11)
                dve.tensor_scalar(logit[:, :], logit[:, :], share[:, :], None, ALU.mult).then_inc(chain, 1)
                dve.wait_ge(chain, 12)
                dve.wait_ge(p_turned, 1)
                dve.tensor_copy(flat(pT), g.bank[2][:, 0:S]).then_inc(pT_ready, 1)
                with dve.Fori(0, NS // 2) as h:
                    for u in range(2):
                        b = 2 * h + u
                        dve.wait_ge(v_used, PG * b + 2 * PG)
                        for half in range(2):
                            rows = slice(half * HD, (half + 1) * HD)
                            src = g.bank[4 + u][rows, half:half + (D // P - 1) * (HB + 2) + 1:HB + 2]
                            dve.tensor_copy(oT[rows, :, ds(b, 1)], src.unsqueeze(2)).then_inc(o_taken, 1)
                dve.wait_ge(new_moved, 16)
                dve.tensor_tensor(heads(v_new[:, :]), heads(v_new[:, :]),
                                  p_new[:, :].unsqueeze(2).broadcast_to([NS, HB, HD]), ALU.mult).then_inc(o_chain, 1)
                dve.wait_ge(o_turned, 1)
                dve.wait_ge(o_chain, 1)
                for a in range(2):
                    cols = slice(a * NB, (a + 1) * NB)
                    dve.tensor_tensor(o[:, cols], v_new[:, cols], g.bank[6 + a][0:NS, :], ALU.add).then_inc(o_chain, 1)


def output_phase(nc, g):
    D, K, NT, NS = g.D, g.K, g.NT, g.NS
    with ExitStack() as st:
        sb = lambda n, s, d=F32: st.enter_context(nc.sbuf_tensor(f"out_{n}", s, d))
        sem = lambda n: g.sem(f"out_{n}")
        w_raw = sb("w_raw", [P, K, D])
        w_hi, w_lo = sb("w_hi", [P, K, D], F32R), sb("w_lo", [P, K, D], F32R)
        gate, gate_s = sb("gate", [P, D]), sb("gate_s", [NS, D])
        o, sg, x, y = ([sb(f"{n}{u}", [P, D]) for u in range(2)] for n in ("o", "sg", "x", "y"))
        oT_hi, oT_lo = ([sb(f"{n}{u}", [P, K, P], F32R) for u in range(2)] for n in ("oT_hi", "oT_lo"))
        w_loaded, w_hi_done, w_ready, gates_loaded = sem("w_loaded"), sem("w_hi_done"), sem("w_ready"), sem("gates_loaded")
        o_loaded = [sem(f"o_loaded{u}") for u in range(2)]
        x_loaded = [sem(f"x_loaded{u}") for u in range(2)]
        og_ready, turned, hi_done, lo_done = sem("og_ready"), sem("turned"), sem("hi_done"), sem("lo_done")
        y_full, y_chain, y_done = sem("y_full"), sem("y_chain"), sem("y_done")
        y_stored = [sem(f"y_stored{u}") for u in range(2)]
        ps_oT = [[g.bank[2 * u + a][:, :].rearrange("p (k c) -> p k c", c=P) for a in range(2)] for u in range(2)]
        ps_y = [g.bank[4 + 2 * u:6 + 2 * u] for u in range(2)]
        y_sample, G0 = g.o.y_sample[:, 0, :], (g.mod_fox + 2 * K) * P

        with nc.Block() as block:
            @block.sync
            def _(sp):
                def load(h, u, rows=P):
                    t = 2 * h + u
                    sample = rows != P
                    part = (lambda a: a) if sample else (lambda a: a[ds(t * P, P), :])
                    sp.wait_ge(turned, t + 1)
                    sp.dma_start(o[u][0:rows, :], part(g.o_fox_s if sample else g.o_fox)).then_inc(o_loaded[u], 16)
                    sp.dma_start(sg[u][0:rows, :], part(g.sg_fox_s if sample else g.sg_fox)).then_inc(o_loaded[u], 16)
                    sp.wait_ge(y_done, t + 1)
                    sp.dma_start(x[u][0:rows, :], part(g.x1_s if sample else g.x1)).then_inc(x_loaded[u], 16)

                def store(h, u):
                    sp.wait_ge(y_done, 2 * h + u + 1 + 2)
                    sp.dma_start(g.o.y_prompt[0, ds((2 * h + u) * P, P), :], y[u][:, :]).then_inc(y_stored[u], 16)

                load(0, 0)
                load(0, 1)
                sp.dma_start(w_raw[:, :, :], g.i.fox_w_out[0].rearrange("(k p) n -> p k n", p=P)).then_inc(w_loaded, 16)
                sp.dma_start(gate[:, :], g.mods[0:1, G0:G0 + D].broadcast_to([P, D])).then_inc(gates_loaded, 16)
                sp.dma_start(gate_s[:, :], g.mods[1:NS + 1, G0:G0 + D]).then_inc(gates_loaded, 16)
                with sp.Fori(0, NT // 2 - 1) as h:
                    for u in range(2):
                        load(h + 1, u)
                        store(h, u)
                load(NT // 2, 0, NS)
                for u in range(2):
                    store(NT // 2 - 1, u)
                sp.wait_ge(y_done, NT + 1 + 2)
                sp.dma_start(y_sample, y[0][0:NS, :]).then_inc(y_stored[0], 16)
                for u in range(2):
                    sp.wait_ge(y_stored[u], 16 * (NT // 2 + 1 + (u == 0)))

            @block.tensor
            def _(pe):
                def turn(h, u):
                    t = 2 * h + u
                    pe.wait_ge(og_ready, t + 1)
                    pe.wait_ge(lo_done, t + 1)
                    for k in range(K):
                        mm = pe.transpose(ps_oT[u][k // 4][:, k % 4, :], o[u][:, k * P:(k + 1) * P], g.ident[:, :])
                    mm.then_inc(turned, 1)

                def project(h, u):
                    t = 2 * h + u
                    pe.wait_ge(lo_done, t + 1 + 2)
                    pe.wait_ge(y_done, t + 1)
                    for a in range(2):
                        cols = slice(a * NB, (a + 1) * NB)
                        for k in range(K):
                            pe.matmul(ps_y[u][a][:, :], oT_hi[u][:, k, :], w_hi[:, k, cols], start=(k == 0), stop=False)
                            pe.matmul(ps_y[u][a][:, :], oT_hi[u][:, k, :], w_lo[:, k, cols], start=False, stop=False)
                            mm = pe.matmul(ps_y[u][a][:, :], oT_lo[u][:, k, :], w_hi[:, k, cols], start=False,
                                           stop=(k == K - 1))
                    mm.then_inc(y_full, 1)

                pe.sem_inc(turned, 2)
                pe.sem_inc(y_full, 2)
                turn(0, 0)
                pe.wait_ge(w_ready, K)
                with pe.Fori(0, NT // 2) as h:
                    turn(h, 1)
                    project(h, 0)
                    turn(h + 1, 0)
                    project(h, 1)
                project(NT // 2, 0)

            @block.scalar
            def _(act):
                def high(h, u):
                    t = 2 * h + u
                    act.wait_ge(turned, t + 1 + 2)
                    act.wait_ge(y_full, t + 1)
                    for a in range(2):
                        act.activation(oT_hi[u][:, 4 * a:4 * a + 4, :], ps_oT[u][a], ACT.Copy).then_inc(hi_done, 1)

                split_output_weight(act, None, w_raw, w_hi, w_lo, w_loaded, w_hi_done, w_ready, K)
                with act.Fori(0, NT // 2) as h:
                    for u in range(2):
                        high(h, u)
                high(NT // 2, 0)

            @block.vector
            def _(dve):
                def gate_o(h, u, rows=P):
                    dve.wait_ge(o_loaded[u], 32 * h + 32)
                    dve.tensor_tensor(o[u][0:rows, :], o[u][0:rows, :], sg[u][0:rows, :], ALU.mult).then_inc(og_ready, 1)

                def low(h, u):
                    t = 2 * h + u
                    dve.wait_ge(y_full, t + 1)
                    for a in range(2):
                        dve.wait_ge(hi_done, 2 * t + a + 1)
                        op = dve.tensor_tensor(oT_lo[u][:, 4 * a:4 * a + 4, :], ps_oT[u][a],
                                               oT_hi[u][:, 4 * a:4 * a + 4, :].bitcast(F32), ALU.subtract)
                    op.then_inc(lo_done, 1)

                def finish(h, u, rows=P):
                    t = 2 * h + u
                    scale = gate if rows == P else gate_s
                    dve.wait_ge(y_full, t + 1 + 2)
                    dve.wait_ge(y_stored[u], 16 * h + 16)
                    for a in range(2):
                        cols = slice(a * NB, (a + 1) * NB)
                        dve.tensor_tensor(y[u][0:rows, cols], ps_y[u][a][0:rows, :], scale[0:rows, cols], ALU.mult)\
                           .then_inc(y_chain, 1)
                    dve.wait_ge(x_loaded[u], 16 * h + 16)
                    dve.wait_ge(y_chain, 2 * t + 2)
                    dve.tensor_tensor(y[u][0:rows, :], y[u][0:rows, :], x[u][0:rows, :], ALU.add).then_inc(y_done, 1)

                dve.sem_inc(lo_done, 2)
                dve.sem_inc(y_done, 2)
                for u in range(2):
                    dve.sem_inc(y_stored[u], 16)
                gate_o(0, 0)
                gate_o(0, 1)
                split_output_weight(None, dve, w_raw, w_hi, w_lo, w_loaded, w_hi_done, w_ready, K)
                dve.wait_ge(gates_loaded, 32)
                low(0, 0)
                with dve.Fori(0, NT // 2 - 1) as h:
                    low(h, 1)
                    gate_o(h + 1, 0)
                    finish(h, 0)
                    low(h + 1, 0)
                    gate_o(h + 1, 1)
                    finish(h, 1)
                h = NT // 2 - 1
                low(h, 1)
                gate_o(h + 1, 0, NS)
                finish(h, 0)
                low(h + 1, 0)
                finish(h, 1)
                finish(h + 1, 0, NS)


def build(nc, inp, out):
    with ExitStack() as ctx:
        g = Names()
        g.i, g.o = inp, out
        g.keep = lambda n, s, d=F32: ctx.enter_context(nc.sbuf_tensor(n, s, d))
        sems = []

        def sem(name):
            sems.append(nc.alloc_semaphore(name))
            return sems[-1]
        g.sem = sem

        def run(phase, *args):
            phase(nc, g, *args)
            nc.clear_and_free_semaphores(sems)
            nc.all_engine_barrier()
            sems.clear()
        g.bank = [ctx.enter_context(nc.psum_tensor(f"bank{b}", [P, NB], F32)) for b in range(8)]
        g.T, g.D = inp.x_prompt.shape[1:]
        g.K, g.NT = g.D // P, g.T // P
        g.NS = inp.x_sample.shape[0]
        g.NA, _, g.HA, g.DK, g.DV = inp.state_gla.shape
        g.POOL, g.PAGE, g.HB, g.HD = inp.cache_k.shape
        g.PAGES = inp.page_table.shape[1]
        g.RANK = inp.gla_w_g2.shape[1]
        assert g.NA == 1 and inp.ada_w.shape[0] == 2 and inp.x_prompt.shape[0] == 1 and inp.x_sample.shape[1] == 1
        assert g.DK == P and g.PAGE == P and g.HB == 16 and 2 * g.HD == P and g.NS * g.HB == P
        T, D, NS, K = g.T, g.D, g.NS, g.K
        dram = lambda n, s: nc.dram_tensor(n, s, F32, kind="Internal").ap()
        n_mods = 2 * inp.ada_w.shape[2] + inp.kv_ada_w.shape[1]
        g.mods = dram("mods", (NS + 1, n_mods))
        g.modT = g.keep("modT", [P, n_mods // P * (NS + 1)], F32)
        g.mod_gla, g.mod_kv, g.mod_fox = 0, 3 * K, 5 * K
        g.mod_scale = [g.mod_gla + K, g.mod_kv + K, g.mod_fox + K]
        g.logf_all = g.keep("logf_all", [P, g.NT * g.HB], F32)
        g.logf_s = g.keep("logf_s", [NS, g.HB], F32)
        QK = g.HA * g.DK
        g.qT, g.kT, g.bT = dram("qT", (QK, T)), dram("kT", (QK, T)), dram("bT", (QK, T))
        g.v_gla, g.sg_gla = dram("v_gla", (T, g.HA * g.DV)), dram("sg_gla", (T, g.HA * g.DV))
        c = g.HA * NS
        g.qT_s, g.kT_s, g.aT_s = dram("qT_s", (P, c)), dram("kT_s", (P, c)), dram("aT_s", (P, c))
        g.v_gla_s, g.sg_gla_s = dram("v_gla_s", (NS, g.HA * g.DV)), dram("sg_gla_s", (NS, g.HA * g.DV))
        g.x1, g.x1_s = dram("x1", (T, D)), dram("x1_s", (NS, D))
        g.q_fox, g.sg_fox, g.o_fox = dram("q_fox", (T, D)), dram("sg_fox", (T, D)), dram("o_fox", (T, D))
        g.f_hi, g.f_lo = dram("f_hi", (g.HB, T)), dram("f_lo", (g.HB, T))
        g.k_rows, g.v_rows = (a[0].rearrange("t h d -> t (h d)") for a in (out.k_prompt, out.v_prompt))
        g.o_fox_s = dram("o_fox_s", (NS, D))
        g.q_fox_s, g.sg_fox_s = dram("q_fox_s", (NS, D)), dram("sg_fox_s", (NS, D))

        run(make_constants)
        run(modulation_phase)
        run(gla_projections)
        run(gla_phase)
        run(kv_projections)
        run(fox_projections)
        run(forget_sums)
        with ExitStack() as st:
            g.scores = st.enter_context(nc.sbuf_tensor("scores", [P, g.PAGES, P], F32))
            g.lf_pages = st.enter_context(nc.sbuf_tensor("lf_pages", [P, g.PAGES, P], F32))
            run(attention_phase)
            run(sample_attention)
        run(output_phase)


def kernel(x_prompt, x_sample, c_prompt, c_sample, state_gla, cache_k, cache_v, cache_logf, page_table, ada_w,
           ada_b, gla_w_in, gla_w_g2, gla_b_g, gla_onorm, gla_w_out, kv_ada_w, kv_ada_b, w_kv, b_f,
           k_norm, fox_w_in, q_norm, fox_w_out):
    import numpy as np
    import concourse.bacc as bacc
    from concourse.bass_utils import run_bass_kernel_spmd

    nc = bacc.Bacc("TRN2", target_bir_lowering=False, num_devices=1)
    arrays, shapes, inp, out = {}, {}, Names(), Names()

    def load(name, a):
        arrays[f"in_{name}"] = a = np.ascontiguousarray(a)
        return nc.dram_tensor(f"in_{name}", a.shape, mybir.dt.from_np(a.dtype), kind="ExternalInput").ap()

    def store(name, shape):
        shapes[name] = shape
        return nc.dram_tensor(f"out_{name}", shape, F32, kind="ExternalOutput").ap()

    inp.x_prompt = load("x_prompt", x_prompt)
    inp.x_sample = load("x_sample", x_sample)
    inp.c_prompt = load("c_prompt", c_prompt)
    inp.c_sample = load("c_sample", c_sample)
    inp.state_gla = load("state_gla", state_gla)
    inp.cache_k = load("cache_k", cache_k)
    inp.cache_v = load("cache_v", cache_v)
    inp.cache_logf = load("cache_logf", cache_logf)
    inp.page_table = load("page_table", page_table)
    inp.ada_w = load("ada_w", ada_w)
    inp.ada_b = load("ada_b", ada_b)
    inp.gla_w_in = load("gla_w_in", gla_w_in)
    inp.gla_w_g2 = load("gla_w_g2", gla_w_g2)
    inp.gla_b_g = load("gla_b_g", gla_b_g)
    inp.gla_onorm = load("gla_onorm", gla_onorm)
    inp.gla_w_out = load("gla_w_out", gla_w_out)
    inp.kv_ada_w = load("kv_ada_w", kv_ada_w)
    inp.kv_ada_b = load("kv_ada_b", kv_ada_b)
    inp.w_kv = load("w_kv", w_kv)
    inp.b_f = load("b_f", b_f)
    inp.k_norm = load("k_norm", k_norm)
    inp.fox_w_in = load("fox_w_in", fox_w_in)
    inp.q_norm = load("q_norm", q_norm)
    inp.fox_w_out = load("fox_w_out", fox_w_out)

    b, t, d = x_prompt.shape
    bs, ts = x_sample.shape[:2]
    na, _, ha, dk, dv = state_gla.shape
    hb, hd = cache_k.shape[2:]
    out.y_prompt = store("y_prompt", (b, t, d))
    out.y_sample = store("y_sample", (bs, ts, d))
    out.state_prompt = store("state_prompt", (na, b, ha, dk, dv))
    out.state_sample = store("state_sample", (na, bs, ha, dk, dv))
    out.k_prompt = store("k_prompt", (b, t, hb, hd))
    out.v_prompt = store("v_prompt", (b, t, hb, hd))
    out.logf_prompt = store("logf_prompt", (b, t, hb))
    out.k_sample = store("k_sample", (bs, ts, hb, hd))
    out.v_sample = store("v_sample", (bs, ts, hb, hd))
    out.logf_sample = store("logf_sample", (bs, ts, hb))
    build(nc, inp, out)
    r = run_bass_kernel_spmd(nc, [arrays], core_ids=[0])
    return tuple(r.results[0][f"out_{name}"] for name in shapes)
```
